# Optimizing a Trainium2 kernel written in Bass

```python
import math
import jax, jax.numpy as jnp
from jax import lax
import numpy as np

D_MODEL = 1024
BATCH = 1
SEQ = 512
DEPTH = 2

DA_HEADS = 4
DA_QK_DIM = 64
DA_V_DIM = 2 * DA_QK_DIM
DA_ROT_DIM = DA_QK_DIM // 4
ROPE_THETA = 500000.0
Q_BLOCK = 128
RET_HEADS = 4
RET_QK_DIM = 32
RET_V_DIM = 2 * RET_QK_DIM
RET_THETA = 10000.0
RET_CHUNK = 128
POOL_GROUPS = 4
POOL_DIM = 64
POOL_WINDOWS = (2, 4, 8, 16)
DA_WIDTH = DA_HEADS * DA_V_DIM
RET_WIDTH = RET_HEADS * RET_V_DIM
POOL_WIDTH = POOL_GROUPS * POOL_DIM
MIX_WIDTH = DA_WIDTH + RET_WIDTH + POOL_WIDTH
SPLIT_SIZES = (DA_HEADS * 2 * DA_QK_DIM, DA_HEADS * 2 * DA_QK_DIM, DA_WIDTH,
               RET_HEADS * RET_QK_DIM, RET_HEADS * RET_QK_DIM, RET_WIDTH, RET_WIDTH,
               POOL_WIDTH)
IN_WIDTH = 2560
D_FF = 2816
CONV_WIDTH = 3
EPS = 1e-6


def rms_norm(x, g):
    xf = x.astype(jnp.float32)
    y = xf * lax.rsqrt(jnp.mean(xf * xf, axis=-1, keepdims=True) + EPS)
    return (y * g).astype(x.dtype)

def rotary(x, pos, rot_dim, theta):
    inv = jnp.float32(theta) ** (-jnp.arange(0, rot_dim, 2, dtype=jnp.float32) / rot_dim)
    ang = pos[:, None] * inv[None, :]
    cos = jnp.cos(ang).astype(x.dtype)
    sin = jnp.sin(ang).astype(x.dtype)
    half = rot_dim // 2
    x1, x2, xp = x[..., :half], x[..., half:rot_dim], x[..., rot_dim:]
    return jnp.concatenate([x1 * cos - x2 * sin, x2 * cos + x1 * sin, xp], axis=-1)

def diff_attention(q, k, v, lq1, lk1, lq2, lk2, subln_g, lam_init):
    B, S, _ = q.shape
    pos = jnp.arange(S, dtype=jnp.float32)
    q = q.reshape(B, S, DA_HEADS, 2, DA_QK_DIM).transpose(0, 2, 3, 1, 4)
    k = k.reshape(B, S, DA_HEADS, 2, DA_QK_DIM).transpose(0, 2, 3, 1, 4)
    q = rotary(q, pos, DA_ROT_DIM, ROPE_THETA)
    k = rotary(k, pos, DA_ROT_DIM, ROPE_THETA)
    v = v.reshape(B, S, DA_HEADS, DA_V_DIM).transpose(0, 2, 1, 3)
    lam = (jnp.exp(jnp.sum(lq1.astype(jnp.float32) * lk1.astype(jnp.float32)))
           - jnp.exp(jnp.sum(lq2.astype(jnp.float32) * lk2.astype(jnp.float32))) + lam_init)
    scale = DA_QK_DIM ** -0.5
    nb = S // Q_BLOCK
    qb = q.reshape(B, DA_HEADS, 2, nb, Q_BLOCK, DA_QK_DIM).transpose(3, 0, 1, 2, 4, 5)
    kpos = jnp.arange(S)

    def block(args):
        q_blk, i = args
        s = jnp.einsum('bhmqd,bhmkd->bhmqk', q_blk, k).astype(jnp.float32) * scale
        qpos = i * Q_BLOCK + jnp.arange(Q_BLOCK)
        mask = kpos[None, :] <= qpos[:, None]
        p = jax.nn.softmax(jnp.where(mask, s, -jnp.inf), axis=-1)
        a = p[:, :, 0] - lam * p[:, :, 1]
        return jnp.einsum('bhqk,bhkd->bhqd', a.astype(v.dtype), v)

    o = lax.map(block, (qb, jnp.arange(nb)))
    o = o.transpose(1, 0, 3, 2, 4).reshape(B, S, DA_HEADS, DA_V_DIM)
    o = rms_norm(o, subln_g) * (1.0 - lam_init)
    return o.reshape(B, S, DA_WIDTH)

def retention(q, k, v, g, ret_g):
    B, S, _ = q.shape
    H, dk, dv, C = RET_HEADS, RET_QK_DIM, RET_V_DIM, RET_CHUNK
    pos = jnp.arange(S, dtype=jnp.float32)
    q = rotary(q.reshape(B, S, H, dk).transpose(0, 2, 1, 3), pos, dk, RET_THETA)
    k = rotary(k.reshape(B, S, H, dk).transpose(0, 2, 1, 3), pos, dk, RET_THETA) * (dk ** -0.5)
    v = v.reshape(B, S, H, dv).transpose(0, 2, 1, 3)
    log_g = jnp.log(1.0 - 2.0 ** (-5.0 - jnp.arange(H, dtype=jnp.float32)))
    idx = jnp.arange(C, dtype=jnp.float32)
    diff = idx[:, None] - idx[None, :]
    decay = jnp.where(diff >= 0, jnp.exp(jnp.maximum(diff, 0.0) * log_g[:, None, None]), 0.0)
    xi = jnp.exp((idx + 1.0) * log_g[:, None])[..., None]
    zeta = jnp.exp((C - 1.0 - idx) * log_g[:, None])[..., None]
    chunk_decay = jnp.exp(C * log_g)[:, None, None]
    nc = S // C

    def to_chunks(t):
        return t.reshape(B, H, nc, C, t.shape[-1]).transpose(2, 0, 1, 3, 4).astype(jnp.float32)

    def step(state, inp):
        qi, ki, vi = inp
        inner = jnp.einsum('bhqd,bhkd->bhqk', qi, ki) * decay
        o = (jnp.einsum('bhqk,bhkv->bhqv', inner, vi)
             + jnp.einsum('bhqd,bhdv->bhqv', qi * xi, state))
        state = state * chunk_decay + jnp.einsum('bhkd,bhkv->bhdv', ki * zeta, vi)
        return state, o

    state0 = jnp.zeros((B, H, dk, dv), jnp.float32)
    _, o = lax.scan(step, state0, (to_chunks(q), to_chunks(k), to_chunks(v)))
    o = o.transpose(1, 0, 3, 2, 4).reshape(B, S, H, dv)
    mu = jnp.mean(o, axis=-1, keepdims=True)
    var = jnp.mean(jnp.square(o - mu), axis=-1, keepdims=True)
    o = (o - mu) * lax.rsqrt(var + EPS) * ret_g.reshape(H, dv)
    return jax.nn.silu(g) * o.reshape(B, S, RET_WIDTH).astype(g.dtype)

def pool_mixer(u, pool_w, pool_scale):
    B, S, _ = u.shape
    ug = u.reshape(B, S, POOL_GROUPS, POOL_DIM).astype(jnp.float32)
    c = jnp.cumsum(ug, axis=1)
    t = jnp.arange(S, dtype=jnp.float32)
    means = []
    for gi, w in enumerate(POOL_WINDOWS):
        cg = c[:, :, gi]
        shifted = jnp.pad(cg, ((0, 0), (w, 0), (0, 0)))[:, :S]
        means.append((cg - shifted) / jnp.minimum(t + 1.0, float(w))[:, None])
    pooled = (jnp.stack(means, axis=2) - ug).astype(u.dtype)
    y = jnp.einsum('bsgp,gpq->bsgq', pooled, pool_w)
    return y.reshape(B, S, POOL_WIDTH) * pool_scale

def conv_mlp(h, w_up, conv_w, conv_b, w_down):
    S = h.shape[1]
    u = h @ w_up
    up = jnp.pad(u, ((0, 0), (CONV_WIDTH - 1, 0), (0, 0)))
    uc = conv_b + sum(conv_w[j] * up[:, j:j + S] for j in range(CONV_WIDTH))
    gate, val = jnp.split(uc, 2, axis=-1)
    return (jax.nn.gelu(gate, approximate=True) * val) @ w_down

def first_inputs(seed: int = 0) -> dict:
    key = jax.random.key(seed)
    ks = jax.random.split(key, 24)
    f32 = jnp.float32

    def nrm(k, shape, scale):
        return jax.random.normal(k, shape, f32) * scale

    def gain(k, shape):
        return 1.0 + 0.05 * jax.random.normal(k, shape, f32)

    L = DEPTH
    return {
        "x": nrm(ks[0], (BATCH, SEQ, D_MODEL), 1.0),
        "norm_mix_pre": gain(ks[1], (L, D_MODEL)),
        "norm_mix_post": gain(ks[2], (L, D_MODEL)),
        "w_in": nrm(ks[3], (L, D_MODEL, IN_WIDTH), D_MODEL ** -0.5),
        "lambda_q1": nrm(ks[4], (L, DA_QK_DIM), 0.1),
        "lambda_k1": nrm(ks[5], (L, DA_QK_DIM), 0.1),
        "lambda_q2": nrm(ks[6], (L, DA_QK_DIM), 0.1),
        "lambda_k2": nrm(ks[7], (L, DA_QK_DIM), 0.1),
        "diff_subln": gain(ks[8], (L, DA_V_DIM)),
        "ret_norm": gain(ks[9], (L, RET_WIDTH)),
        "pool_w": nrm(ks[10], (L, POOL_GROUPS, POOL_DIM, POOL_DIM), POOL_DIM ** -0.5),
        "pool_scale": 0.5 + 0.1 * jax.random.normal(ks[11], (L, POOL_WIDTH), f32),
        "w_out": nrm(ks[12], (L, MIX_WIDTH, D_MODEL), MIX_WIDTH ** -0.5),
        "norm_mlp_pre": gain(ks[13], (L, D_MODEL)),
        "norm_mlp_post": gain(ks[14], (L, D_MODEL)),
        "w_up": nrm(ks[15], (L, D_MODEL, 2 * D_FF), D_MODEL ** -0.5),
        "conv_w": nrm(ks[16], (L, CONV_WIDTH, 2 * D_FF), CONV_WIDTH ** -0.5),
        "conv_b": nrm(ks[17], (L, 2 * D_FF), 0.02),
        "w_down": nrm(ks[18], (L, D_FF, D_MODEL), D_FF ** -0.5),
    }

def first_block(x, norm_mix_pre, norm_mix_post, w_in, lambda_q1, lambda_k1, lambda_q2, lambda_k2,
              diff_subln, ret_norm, pool_w, pool_scale, w_out, norm_mlp_pre, norm_mlp_post,
              w_up, conv_w, conv_b, w_down):
    split_points = []
    acc = 0
    for s in SPLIT_SIZES[:-1]:
        acc += s
        split_points.append(acc)
    for l in range(DEPTH):
        lam_init = 0.8 - 0.6 * math.exp(-0.3 * l)
        h = rms_norm(x, norm_mix_pre[l])
        proj = h @ w_in[l]
        q_da, k_da, v_da, q_r, k_r, v_r, g_r, u_pool = jnp.split(proj, split_points, axis=-1)
        o_da = diff_attention(q_da, k_da, v_da, lambda_q1[l], lambda_k1[l], lambda_q2[l],
                              lambda_k2[l], diff_subln[l], lam_init)
        o_ret = retention(q_r, k_r, v_r, g_r, ret_norm[l])
        o_pool = pool_mixer(u_pool, pool_w[l], pool_scale[l])
        mix = jnp.concatenate([o_da, o_ret, o_pool], axis=-1) @ w_out[l]
        x = x + rms_norm(mix, norm_mix_post[l])
        h = rms_norm(x, norm_mlp_pre[l])
        y = conv_mlp(h, w_up[l], conv_w[l], conv_b[l], w_down[l])
        x = x + rms_norm(y, norm_mlp_post[l])
    return x


N_META = 16
GRID_W = 64
GLA_HEADS = 4
GLA_DK = 64
GLA_DV = 128
GLA_KEY = GLA_HEADS * GLA_DK
GLA_VAL = GLA_HEADS * GLA_DV
GLA_RANK = 16
GLA_TAU = 16.0
CHUNK = 64
ATT_HEADS = 8
ATT_KV_HEADS = 2
HEAD_DIM = 64
ATT_Q = ATT_HEADS * HEAD_DIM
ATT_KV = ATT_KV_HEADS * HEAD_DIM
ROPE_THETA_2 = 10000.0

IN_SIZES = (GLA_KEY, GLA_KEY, GLA_VAL, GLA_VAL, GLA_RANK, GLA_RANK,
            ATT_Q, ATT_KV, ATT_KV, D_MODEL, D_MODEL)
D_IN = sum(IN_SIZES)
SPLIT_POINTS = tuple(int(s) for s in np.cumsum(IN_SIZES)[:-1])


def rmsnorm(x, g):
    xf = x.astype(jnp.float32)
    y = xf * lax.rsqrt(jnp.mean(xf * xf, axis=-1, keepdims=True) + EPS)
    return (y * g.astype(jnp.float32)).astype(x.dtype)

def swiglu(x, w_gate, w_up, w_down):
    return (jax.nn.silu(x @ w_gate) * (x @ w_up)) @ w_down

def gla_causal_chunked(q, k, v, log_a):
    f32 = jnp.float32
    B, H, T, dk = q.shape
    dv = v.shape[-1]
    n = T // CHUNK
    qc = q.astype(f32).reshape(B, H, n, CHUNK, dk)
    kc = k.astype(f32).reshape(B, H, n, CHUNK, dk)
    vc = v.astype(f32).reshape(B, H, n, CHUNK, dv)
    bcum = jnp.cumsum(log_a.astype(f32).reshape(B, H, n, CHUNK, dk), axis=3)
    btot = bcum[:, :, :, -1:, :]
    q_dec = qc * jnp.exp(bcum)
    k_inv = kc * jnp.exp(-bcum)
    k_end = kc * jnp.exp(btot - bcum)
    mask = jnp.tril(jnp.ones((CHUNK, CHUNK), dtype=bool))
    att = jnp.where(mask, jnp.einsum('bhnid,bhnjd->bhnij', q_dec, k_inv), 0.0)
    o_intra = jnp.einsum('bhnij,bhnjv->bhniv', att, vc)
    kv_chunk = jnp.einsum('bhnjd,bhnjv->bhndv', k_end, vc)
    decay = jnp.exp(btot[:, :, :, 0, :])

    def step(S, inp):
        d, kv = inp
        return d[..., None] * S + kv, S

    S0 = jnp.zeros((B, H, dk, dv), f32)
    _, S_prev = lax.scan(step, S0, (jnp.moveaxis(decay, 2, 0), jnp.moveaxis(kv_chunk, 2, 0)))
    S_prev = jnp.moveaxis(S_prev, 0, 2)
    o_inter = jnp.einsum('bhnid,bhndv->bhniv', q_dec, S_prev)
    return (o_intra + o_inter).reshape(B, H, T, dv)

def gla_branch(q, k, v, r, lr_f, lr_b, w2, b2, gn_gain):
    B, L, _ = q.shape
    pad = CHUNK - N_META

    def heads(t, d):
        return t.reshape(B, L, GLA_HEADS, d).transpose(0, 2, 1, 3)

    def log_gate(lr, w, b):
        return jax.nn.log_sigmoid((lr @ w + b).astype(jnp.float32)) / GLA_TAU

    def padseq(t):
        return jnp.pad(t, ((0, 0), (0, 0), (pad, 0), (0, 0)))

    def flip(t):
        return jnp.flip(t, axis=2)

    qh = padseq(heads(q * GLA_DK ** -0.5, GLA_DK))
    kh = padseq(heads(k, GLA_DK))
    vh = padseq(heads(v, GLA_DV))
    gf = padseq(heads(log_gate(lr_f, w2[0], b2[0]), GLA_DK))
    gb = padseq(heads(log_gate(lr_b, w2[1], b2[1]), GLA_DK))
    o_f = gla_causal_chunked(qh, kh, vh, gf)
    o_b = flip(gla_causal_chunked(flip(qh), flip(kh), flip(vh), flip(gb)))
    o = (o_f + o_b)[:, :, pad:, :].transpose(0, 2, 1, 3)
    o = o * lax.rsqrt(jnp.mean(o * o, axis=-1, keepdims=True) + EPS)
    o = o.reshape(B, L, GLA_VAL) * gn_gain.astype(jnp.float32)
    return o.astype(r.dtype) * jax.nn.silu(r)

def axial_rope_tables(n_tok):
    f32 = jnp.float32
    rows = n_tok // GRID_W
    row = jnp.repeat(jnp.arange(rows), GRID_W).astype(f32)
    col = jnp.tile(jnp.arange(GRID_W), rows).astype(f32)
    axis_dim = HEAD_DIM // 2
    inv = ROPE_THETA_2 ** (-jnp.arange(0, axis_dim, 2, dtype=f32) / axis_dim)
    ang = jnp.concatenate([row[:, None] * inv, col[:, None] * inv], axis=-1)
    ang = jnp.concatenate([jnp.zeros((N_META, axis_dim), f32), ang], axis=0)
    return jnp.cos(ang), jnp.sin(ang)

def apply_axial_rope(x, cos, sin):
    L = x.shape[-2]
    q4 = HEAD_DIM // 4
    xs = x.astype(jnp.float32).reshape(*x.shape[:-1], 2, 2, q4)
    x1, x2 = xs[..., 0, :], xs[..., 1, :]
    c = cos.reshape(L, 2, q4)
    s = sin.reshape(L, 2, q4)
    return jnp.stack([x1 * c - x2 * s, x2 * c + x1 * s], axis=-2).reshape(x.shape)

def attention_branch(q, k, v, gq, gk, cos, sin):
    B, L, _ = q.shape
    G = ATT_HEADS // ATT_KV_HEADS
    qh = q.reshape(B, L, ATT_KV_HEADS, G, HEAD_DIM).transpose(0, 2, 3, 1, 4)
    kh = k.reshape(B, L, ATT_KV_HEADS, HEAD_DIM).transpose(0, 2, 1, 3)
    vh = v.reshape(B, L, ATT_KV_HEADS, HEAD_DIM).transpose(0, 2, 1, 3)
    qh = apply_axial_rope(rmsnorm(qh, gq), cos, sin) * HEAD_DIM ** -0.5
    kh = apply_axial_rope(rmsnorm(kh, gk), cos, sin)
    pad = Q_BLOCK - N_META
    qp = jnp.pad(qh, ((0, 0), (0, 0), (0, 0), (pad, 0), (0, 0)))
    nblk = qp.shape[3] // Q_BLOCK
    qb = jnp.moveaxis(qp.reshape(B, ATT_KV_HEADS, G, nblk, Q_BLOCK, HEAD_DIM), 3, 0)

    def block(qblk):
        s = jnp.einsum('bkgqd,bksd->bkgqs', qblk, kh)
        p = jax.nn.softmax(s, axis=-1)
        return jnp.einsum('bkgqs,bksd->bkgqd', p.astype(vh.dtype), vh)

    o = lax.map(block, qb)
    o = jnp.moveaxis(o, 0, 3).reshape(B, ATT_KV_HEADS, G, nblk * Q_BLOCK, HEAD_DIM)[:, :, :, pad:]
    return o.transpose(0, 3, 1, 2, 4).reshape(B, L, ATT_Q).astype(q.dtype)

def mixer(z, w_in, gla_w2, gla_b2, gla_gn, q_norm, k_norm, w_pa, w_pb, b_merge, w_out, cos, sin):
    h = z @ w_in
    (q_a, k_a, v_a, r_a, lr_f, lr_b, q_b, k_b, v_b, g_a, g_b) = jnp.split(h, SPLIT_POINTS, axis=-1)
    a = gla_branch(q_a, k_a, v_a, r_a, lr_f, lr_b, gla_w2, gla_b2, gla_gn)
    b = attention_branch(q_b, k_b, v_b, q_norm, k_norm, cos, sin)
    y = (jax.nn.sigmoid(g_a + b_merge[0]) * (a @ w_pa)
         + jax.nn.sigmoid(g_b + b_merge[1]) * (b @ w_pb))
    return y @ w_out

def second_inputs(seed: int = 0) -> dict:
    key = jax.random.key(seed)
    ks = jax.random.split(key, 18)

    def nrm(k, shape, scale):
        return jax.random.normal(k, shape, jnp.float32) * scale

    return {
        "x": nrm(ks[0], (BATCH, SEQ, D_MODEL), 1.0),
        "meta_tokens": nrm(ks[1], (N_META, D_MODEL), 1.0),
        "norm_gains": 1.0 + nrm(ks[2], (DEPTH, 3, D_MODEL), 0.02),
        "ffn_w_gate": nrm(ks[3], (DEPTH, 2, D_MODEL, D_FF), D_MODEL ** -0.5),
        "ffn_w_up": nrm(ks[4], (DEPTH, 2, D_MODEL, D_FF), D_MODEL ** -0.5),
        "ffn_w_down": nrm(ks[5], (DEPTH, 2, D_FF, D_MODEL), D_FF ** -0.5),
        "w_in": nrm(ks[6], (DEPTH, D_MODEL, D_IN), D_MODEL ** -0.5),
        "gla_w2": nrm(ks[7], (DEPTH, 2, GLA_RANK, GLA_KEY), GLA_RANK ** -0.5),
        "gla_b2": nrm(ks[8], (DEPTH, 2, GLA_KEY), 0.1),
        "gla_gn": 1.0 + nrm(ks[9], (DEPTH, GLA_VAL), 0.02),
        "q_norm": 1.0 + nrm(ks[10], (DEPTH, HEAD_DIM), 0.02),
        "k_norm": 1.0 + nrm(ks[11], (DEPTH, HEAD_DIM), 0.02),
        "w_pa": nrm(ks[12], (DEPTH, GLA_VAL, D_MODEL), GLA_VAL ** -0.5),
        "w_pb": nrm(ks[13], (DEPTH, ATT_Q, D_MODEL), ATT_Q ** -0.5),
        "b_merge": nrm(ks[14], (DEPTH, 2, D_MODEL), 0.02),
        "w_out": nrm(ks[15], (DEPTH, D_MODEL, D_MODEL), D_MODEL ** -0.5),
        "final_norm": 1.0 + nrm(ks[16], (D_MODEL,), 0.02),
    }

def second_block(x, meta_tokens, norm_gains, ffn_w_gate, ffn_w_up, ffn_w_down, w_in, gla_w2, gla_b2,
              gla_gn, q_norm, k_norm, w_pa, w_pb, b_merge, w_out, final_norm):
    B, N, D = x.shape
    meta = jnp.broadcast_to(meta_tokens[None].astype(x.dtype), (B, N_META, D))
    h = jnp.concatenate([meta, x], axis=1)
    cos, sin = axial_rope_tables(N)
    for l in range(DEPTH):
        h = h + 0.5 * swiglu(rmsnorm(h, norm_gains[l, 0]),
                             ffn_w_gate[l, 0], ffn_w_up[l, 0], ffn_w_down[l, 0])
        h = h + mixer(rmsnorm(h, norm_gains[l, 1]), w_in[l], gla_w2[l], gla_b2[l], gla_gn[l],
                      q_norm[l], k_norm[l], w_pa[l], w_pb[l], b_merge[l], w_out[l], cos, sin)
        h = h + 0.5 * swiglu(rmsnorm(h, norm_gains[l, 2]),
                             ffn_w_gate[l, 1], ffn_w_up[l, 1], ffn_w_down[l, 1])
    return rmsnorm(h, final_norm)[:, N_META:]


def setup_inputs(seed=0):
    out = dict(first_inputs(seed))
    for name, value in second_inputs(seed + 1).items():
        if name != "x":
            out[name + "_2"] = value
    return out


def reference(
    x, norm_mix_pre, norm_mix_post, w_in, lambda_q1, lambda_k1, lambda_q2, lambda_k2,
    diff_subln, ret_norm, pool_w, pool_scale, w_out, norm_mlp_pre, norm_mlp_post, w_up, conv_w,
    conv_b, w_down, meta_tokens_2, norm_gains_2, ffn_w_gate_2, ffn_w_up_2, ffn_w_down_2, w_in_2,
    gla_w2_2, gla_b2_2, gla_gn_2, q_norm_2, k_norm_2, w_pa_2, w_pb_2, b_merge_2, w_out_2,
    final_norm_2,
):
    x = first_block(
        x, norm_mix_pre, norm_mix_post, w_in, lambda_q1, lambda_k1, lambda_q2, lambda_k2,
        diff_subln, ret_norm, pool_w, pool_scale, w_out, norm_mlp_pre, norm_mlp_post, w_up,
        conv_w, conv_b, w_down,
    )
    return second_block(
        x, meta_tokens_2, norm_gains_2, ffn_w_gate_2, ffn_w_up_2, ffn_w_down_2, w_in_2,
        gla_w2_2, gla_b2_2, gla_gn_2, q_norm_2, k_norm_2, w_pa_2, w_pb_2, b_merge_2, w_out_2,
        final_norm_2,
    )


_drawn_inputs = setup_inputs


def setup_inputs(seed=0):
    import zlib

    import numpy as np

    out = dict(_drawn_inputs(seed))
    spreads = {}
    factors = {'meta_tokens_2': 3.312,
     'norm_gains_2': 4.562,
     'gla_b2_2': 5.688,
     'gla_gn_2': 8.0,
     'q_norm_2': 8.0,
     'k_norm_2': 8.0,
     'b_merge_2': 8.0,
     'final_norm_2': 2.731}
    for name, (base, spread) in spreads.items():
        noise = np.random.default_rng([zlib.crc32(name.encode()), seed]).standard_normal(out[name].shape)
        drawn = base * np.exp(spread * noise) if base else spread * noise
        out[name] = __import__('jax').numpy.asarray(drawn.astype(out[name].dtype))
    for name, factor in factors.items():
        out[name] = (out[name] * factor).astype(out[name].dtype)
    return out
```

```python
import math
from contextlib import ExitStack, contextmanager

import numpy as np

import concourse.bass as bass
from concourse import mybir

F32 = mybir.dt.float32
F32R = mybir.dt.float32r
ALU = mybir.AluOpType
ACT = mybir.ActivationFunctionType
AX_X = mybir.AxisListType.X

P = 128
D = 1024
KT = D // P
SEQ = 512
META = 16
TALL = SEQ + META
HALF = TALL // 2
LAYERS = 2
FF = 2816
FT = FF // P
EPS = 1e-6
SW = KT * P

IN1, OUT1 = 20, 8
LAYER1 = IN1 + OUT1 + 2 * FT + 3 * KT
IN2 = 20
MERGE2 = 3 * KT
FFN2 = 2 * FT + 3 * KT
LAYER2 = FFN2 + IN2 + MERGE2 + KT + FFN2
STRIPS = LAYERS * (LAYER1 + LAYER2)

C_PRE, C_POST, C_SUB, C_RETG, C_PSC, C_MPRE, C_MPOST = 0, 8, 16, 17, 19, 21, 29
C_CW = 37
C_CB = C_CW + 3 * 2 * FT
C_LAM = C_CB + 2 * FT
C_LINIT = C_LAM + 4
C_PW = C_LINIT + 2
NP1 = C_PW + 128
G_N, G_GN, G_QN, G_KN, G_BM = 0, 24, 28, 29, 30
G_W2 = 46
NP2 = G_W2 + 512
K_ID, K_ONES, K_ONE128, K_BLK, K_PDA, K_PR, K_CAUS, K_REC = 0, 128, 256, 384, 512, 640, 768, 1024
NC1 = K_REC + 32 + 2
K2_PQ, K2_E0, K2_E1, K2_S0, K2_S1, K2_CF, K2_CB = 512, 640, 768, 896, 1024, 1152, 1280
NC2 = 1408
TB1 = 4 * SEQ + 4 * SEQ
TB2 = 2 * TALL + 512

TILES2 = [(0, META)] + [(META + P * i, P) for i in range(4)]
QB = 88
NQB = TALL // QB


class Tally:

    def __init__(self, start=0):
        self.n, self.loops = start, []

    def up(self, k=1):
        self.n += k
        return self.now()

    def now(self):
        v = self.n
        for reg, per in self.loops:
            v = reg * per + v
        return v


SETTLED = []


def settle(eng):
    eng.sem_inc(SETTLED[0], 1)


@contextmanager
def loop(eng, trips, events):
    starts = [t.n for t, _ in events]
    settle(eng)
    with eng.Fori(0, trips) as i:
        for t, per in events:
            t.loops.append((i, per))
        yield i
        for (t, _), s in zip(events, starts):
            t.loops.pop()
    got = [t.n - s for (t, _), s in zip(events, starts)]
    assert got == [per for _, per in events], (got, [per for _, per in events])
    for (t, per), s in zip(events, starts):
        t.n = s + per * trips


PER_LAYER = {
    ('Activation', 0): (
        768, 768, 96, 0, 80, 32, 4, 4, 16, 0, 22, 0, 22, 6, 2, 6, 6, 16, 16, 16, 4, 6, 1, 2,
        0, 0, 0, 0, 0, 0, 8, 0, 48, 22),
    ('Activation', 1): (
        1504, 1504, 188, 0, 156, 66, 3, 3, 0, 0, 0, 0, 52, 11, 0, 9, 9, 48, 48, 0, 0, 4, 0, 0,
        4, 4, 5, 6, 4, 5, 10, 1, 48, 52),
    ('DVE', 0): (
        96, 96, 96, 0, 80, 16, 16, 32, 32, 4, 16, 169, 44, 22, 22, 22, 22, 22, 10, 10, 10, 32, 16, 16,
        2, 2, 2, 6, 2, 6, 8, 8, 2, 2, 2, 1, 16, 16, 16, 16, 4, 48, 0, 0, 0, 0, 0, 0,
        0, 0, 0, 0, 0, 0, 16, 16, 16, 0, 0),
    ('DVE', 1): (
        188, 188, 188, 0, 156, 24, 24, 24, 24, 3, 0, 179, 0, 0, 60, 52, 52, 52, 6, 0, 6, 48, 0, 0,
        0, 0, 0, 9, 4, 4, 10, 10, 0, 0, 0, 0, 48, 0, 0, 48, 0, 48, 5, 5, 4, 4, 4, 4,
        10, 10, 10, 2, 4, 5, 48, 48, 48, 6, 1),
    ('Pool', 0): (
        80, 32, 0, 16, 16, 48, 1, 0, 10, 2, 12, 22, 22, 22),
    ('Pool', 1): (
        156, 24, 0, 0, 0, 48, 1, 0, 6, 0, 0, 52, 52, 52),
    ('PE', 0): (
        96, 96, 80, 32, 4, 0, 16, 22, 8, 6, 2, 1, 10, 16, 16, 2, 6, 6, 2, 16, 16, 16, 16, 4,
        0, 0, 0, 0, 0, 0, 0, 0, 0, 16, 0, 48, 0),
    ('PE', 1): (
        188, 188, 156, 24, 3, 0, 24, 52, 10, 11, 0, 0, 6, 0, 0, 0, 9, 9, 0, 48, 0, 48, 48, 0,
        5, 4, 0, 4, 10, 10, 4, 0, 5, 48, 6, 48, 4),
}
MEASURED = {}


def build(nc, weights, params1, params2, consts1, consts2, tables1, tables2, x_in, meta_in, fnorm, out, stop=None):
    with ExitStack() as ctx:
        def sb(name, shape, dt=F32, c=ctx):
            return c.enter_context(nc.sbuf_tensor(name, shape, dt))

        def sem(name):
            return ctx.enter_context(nc.semaphore(name))

        x = sb("x", [P, KT, TALL])
        stage = [sb(f"stage{i}", [P, SW]) for i in range(2)]
        whi = [sb(f"w_hi{i}", [P, SW], F32R) for i in range(2)]
        wlo = [sb(f"w_lo{i}", [P, SW], F32R) for i in range(2)]
        xh = sb("x_hi", [P, KT, TALL], F32R)
        xl = sb("x_lo", [P, KT, TALL], F32R)
        rB = sb("r_tokens", [P, TALL])
        rY = sb("r_post", [P, TALL])
        ss = sb("sumsq", [P, TALL])
        sq = sb("squares", [P, 2, TALL])
        par = sb("params", [P, max(NP1, NP2)])
        con = sb("consts", [P, NC2])
        fng = sb("final_gain", [P, KT])
        eps_one = sb("eps_and_one", [P, 2])
        first_use = sb("first_use", [P, 1])
        with ExitStack() as c:
            fh = sb("ff_hi", [P, FT, TALL], F32R, c)
            fl = sb("ff_lo", [P, FT, TALL], F32R, c)
            Yf = sb("y_mlp", [P, KT, SEQ], F32, c)
            G = sb("gate", [P, TALL], F32, c)
            U = sb("up", [P, TALL], F32, c)
            V = sb("tap", [P, TALL], F32, c)
        with ExitStack() as c:
            PR = sb("proj1", [P, IN1, SEQ], F32, c)
            VT = sb("v_tokens1", [P, 4, SEQ], F32, c)
            VR = sb("vr_tokens", [P, 4, 256], F32, c)
            tb1 = sb("rotary_decay", [P, TB1], F32, c)
            PB = sb("probs1", [P, 2, 2, SEQ], F32, c)
            AT = sb("probsT1", [P, 2, SEQ], F32, c)
            RC = sb("rot_cos1", [P, 2, SEQ], F32, c)
            RS = sb("rot_sin1", [P, 2, SEQ], F32, c)
            MX = sb("maxima1", [P, 2, 8], F32, c)
            WS = sb("window_sums", [P, 2, 2, SEQ], F32, c)
            lam = sb("lambda", [P, 8], F32, c)
        with ExitStack() as c:
            mh = sb("mix_hi", [P, KT, TALL], F32R, c)
            ml = sb("mix_lo", [P, KT, TALL], F32R, c)
            tb2 = sb("rotary_masks", [P, TB2], F32, c)
            with ExitStack() as cc:
                PR2 = sb("proj2", [P, 18, TALL], F32, cc)
                with ExitStack() as c3:
                    VA = sb("va_tokens", [P, 5, 512], F32, c3)
                    LG = sb("log_gates", [P, 5, 512], F32, c3)
                    QD = sb("q_decayed", [P, 4, TALL], F32, c3)
                    KI = sb("k_undecayed", [P, 4, TALL], F32, c3)
                    DC = sb("chunk_decay", [P, 4, 9], F32, c3)
                with ExitStack() as c3:
                    VB = sb("vb_tokens", [P, 5, P], F32, c3)
                    K2 = sb("k_both", [P, 2, TALL], F32, c3)
                    PB2 = sb("probs2", [P, 2, TALL], F32, c3)
                    PT2 = sb("probsT2", [P, 2, 5, QB], F32, c3)
                    MX2 = sb("maxima2", [P, 2, 2], F32, c3)
                    SU2 = sb("sums2", [P, 2, 8], F32, c3)
                    RI2 = sb("inverse_sums2", [P, 2, 8], F32, c3)
                    OB = sb("out_tokens", [P, 2, 512], F32, c3)
            with ExitStack() as cc:
                yh = sb("y_hi", [P, KT, TALL], F32R, cc)
                yl = sb("y_lo", [P, KT, TALL], F32R, cc)
                G0 = sb("sig_a", [P, TALL], F32, cc)
                G1 = sb("sig_b", [P, TALL], F32, cc)
                T0 = sb("merged", [P, TALL], F32, cc)
        E1, E2 = sq[:, 0, :], sq[:, 1, :]
        LR = rY
        acc = [ctx.enter_context(nc.psum_tensor(f"acc{i}", [P, 2, 512], F32)) for i in range(2)]
        M = ctx.enter_context(nc.psum_tensor("misc", [P, 4, 512], F32))

        def view(bank_pair, T, n=P):
            return bank_pair[0:n, 0, 0:T] if T == SEQ else bank_pair[0:n, :, 0:HALF]

        def like(ap, T):
            return ap if T == SEQ else ap.rearrange("p (h t) -> p h t", h=2)

        def tile_of(buf, m, T):
            if isinstance(m, int):
                return buf[:, m, 0:T]
            return buf[:, bass.ds(m, 1), 0:T].rearrange("p o t -> p (o t)")

        def xs(m, T):
            if isinstance(m, int):
                return x[:, m, TALL - T:]
            return x[:, bass.ds(m, 1), TALL - T:].rearrange("p o t -> p (o t)")

        def gain(c, i=0):
            if isinstance(i, int):
                return par[:, c + i:c + i + 1]
            return par[:, bass.ds(i + c, 1)]

        def halves(T):
            return [(0, 0, SEQ)] if T == SEQ else [(0, 0, HALF), (1, HALF, HALF)]

        staged = [sem(f"staged{i}") for i in range(2)]
        hi_ready = sem("hi_ready")
        lo_ready = sem("lo_ready")
        strip_done = sem("strip_done")
        evacuated = sem("evacuated")
        xh_ready, xl_ready = sem("xh_ready"), sem("xl_ready")
        sq_ready = sem("sq_ready")
        ss_added = sem("ss_added")
        stats_full = sem("stats_full")
        r_ready = sem("r_ready")
        y_scaled = sem("y_scaled")
        x_ready = sem("x_ready")
        tap_ready = sem("tap_ready")
        conv_done = sem("conv_done")
        gate_act = sem("gate_act")
        prod_ready = sem("prod_ready")
        fh_ready, ff_ready = sem("fh_ready"), sem("ff_ready")
        param_in = sem("param_in")
        x_in_sem = sem("x_in")
        layer_done = sem("layer_done")
        act_step, dve_step, pool_step, pe_step = sem("act_step"), sem("dve_step"), sem("pool_step"), sem("pe_step")
        out_sem, out_ready = sem("out_sem"), sem("out_ready")
        tr_full, tr_done = sem("tr_full"), sem("tr_done")
        cos_ready = sem("cos_ready")
        rot_full, roped = sem("rot_full"), sem("roped")
        sc_full, st_ready, st_used = sem("sc_full"), sem("st_ready"), sem("st_used")
        o_full, o_sb, mean_full = sem("o_full"), sem("o_sb"), sem("mean_full")
        osq_ready, ovar_full, rg_ready = sem("osq_ready"), sem("ovar_full"), sem("rg_ready")
        silu_ready, o_ready, mh_ready, ml_ready = sem("silu_ready"), sem("o_ready"), sem("mh_ready"), sem("ml_ready")
        pooled, win_ready, pool_full = sem("pooled"), sem("win_ready"), sem("pool_full")
        lam_in, lam_full, lam_exp = sem("lam_in"), sem("lam_full"), sem("lam_exp")
        max_ready, exp_ready, a_ready = sem("max_ready"), sem("exp_ready"), sem("a_ready")
        at_full, at_ready, av_done, o_evac = sem("at_full"), sem("at_ready"), sem("av_done"), sem("o_evac")
        centred, half_bias, consts_in = sem("centred"), sem("half_bias"), sem("consts_in")
        z_full, lnz_ready, lg_ready, cum_full = sem("z_full"), sem("lnz_ready"), sem("lg_ready"), sem("cum_full")
        e_ready, e_used, kv_full, state_ready = sem("e_ready"), sem("e_used"), sem("kv_full"), sem("state_ready")
        att_full, att_ready, att_used, go_full = sem("att_full"), sem("att_ready"), sem("att_used"), sem("go_full")
        go_evac, qn_ready, ob_ready, ot_full = sem("go_evac"), sem("qn_ready"), sem("ob_ready"), sem("ot_full")
        SS = PR2[:, 4:8, :].rearrange("p a t -> p (a t)")[:, 0:16 * P].rearrange("p (d s) -> p d s", d=2)
        ATG = PR2[:, 2:4, :].rearrange("p a t -> p (a t)")[:, 0:8 * P].rearrange("p (b s) -> p b s", b=2)
        SETTLED[:] = [sem("settled")]
        def z_bank(t, n):
            return (M[0:n, 0, :], M[0:n, 1, :], acc[0][0:n, 0, :], acc[0][0:n, 1, :], acc[1][0:n, 0, :])[t]

        eps_c, one_c = eps_one[:, 0:1], eps_one[:, 1:2]

        now_layer = [0]

        def run_layers(eng, f1, f2, tallies):
            for kind, f in enumerate((f1, f2)):
                key = (str(eng.engine).split(".")[-1], kind)
                per = PER_LAYER.get(key) or (0,) * len(tallies)
                starts = [t.n for t in tallies]
                with eng.Fori(0, LAYERS) as i:
                    now_layer[0] = i
                    for t, k in zip(tallies, per):
                        t.loops.append((i, k)) if k else None
                    f()
                    for t, k in zip(tallies, per):
                        t.loops.pop() if k else None
                got = tuple(t.n - s for t, s in zip(tallies, starts))
                MEASURED[key] = got
                for t, s, k in zip(tallies, starts, got):
                    t.n = s + k * LAYERS

        block = ctx.enter_context(nc.Block())

        @block.sync
        def _(sp):
            sp.dma_start(x[:, :, META:], x_in).then_inc(x_in_sem, 16)
            sp.dma_start(x[:, :, 0:META], meta_in).then_inc(x_in_sem, 16)
            sp.dma_start(fng[:, :], fnorm).then_inc(x_in_sem, 16)
            for p in range(2):
                sp.dma_start(stage[p][:, :], weights[p]).then_inc(staged[p], 16)
            with sp.Fori(0, (STRIPS - 2) // 2) as i:
                for p in range(2):
                    sp.wait_ge(lo_ready, 2 * i + (p + 1))
                    sp.dma_start(stage[p][:, :], weights[2 * i + (2 + p)]).then_inc(staged[p], 16)
            for p in range(2):
                sp.wait_ge(lo_ready, STRIPS - 1 + p)
                sp.dma_start(stage[p][:, :], weights[p]).then_inc(staged[p], 16)
            sp.wait_ge(out_ready, KT)
            sp.dma_start(out, x[:, :, META:]).then_inc(out_sem, 16)
            sp.wait_ge(out_sem, 16)

        @block.scalar
        def _(act):
            stg = [Tally(), Tally()]
            free, data, ev = Tally(), Tally(2), Tally(2)
            hi_n, steps = Tally(), Tally()
            stats, yr, xr = Tally(), Tally(1), Tally()
            tap, conv, ga, prod, xin, prm = Tally(), Tally(), Tally(), Tally(), Tally(), Tally()
            trf, cen, ovf, rg, mx, atf, av, oe, orr, olm, pf, cumf, eu, zf, obt = (
                Tally(), Tally(), Tally(), Tally(), Tally(), Tally(2), Tally(), Tally(2), Tally(), Tally(),
                Tally(), Tally(), Tally(), Tally(), Tally())
            strip = [0]

            def chain(ins):
                ins.then_inc(act_step, 1)
                act.wait_ge(act_step, steps.up())

            def split_hi():
                p = strip[0] % 2
                strip[0] += 1
                act.wait_ge(staged[p], stg[p].up(16))
                act.wait_ge(strip_done, free.up())
                nc.scalar.copy(whi[p][:, :], stage[p][:, :]).then_inc(hi_ready, 1)

            def wait_evacuated(k=1):
                act.wait_ge(evacuated, ev.up(k))

            def inverse_rms(dst, src, sem_, tally):
                chain(nc.scalar.activation(dst, src, ACT.Ln, bias=eps_c[0:dst.shape[0], :]))
                nc.scalar.activation(dst, dst, ACT.Exp, scale=-0.5).then_inc(sem_, 1)
                act.wait_ge(sem_, tally.up())

            def choose_table(function):
                chain(nc.scalar.activation(first_use[:, :], eps_c, function))

            def inverse_rms_pair(parts, sem_, tally):
                for dst, src in parts:
                    act.wait_ge(ovar_full, ovf.up())
                    nc.scalar.activation(dst, src, ACT.Ln, bias=eps_c[0:dst.shape[0], :]).then_inc(act_step, 1)
                    steps.up()
                act.wait_ge(act_step, steps.now())
                for dst, src in parts:
                    nc.scalar.activation(dst, dst, ACT.Exp, scale=-0.5).then_inc(sem_, 1)
                act.wait_ge(sem_, tally.up(len(parts)))

            def norm_in(T, gcol, updated):
                for m in range(KT):
                    if updated:
                        act.wait_ge(x_ready, xr.up())
                    nc.scalar.activation(xh[:, m, 0:T], xs(m, T), ACT.Copy, scale=gain(gcol, m)).then_inc(xh_ready, 1)
                act.wait_ge(stats_full, stats.up())
                inverse_rms(like(rB[:, 0:T], T), view(M[:, 0:2, :], T), r_ready, yr)

            def post_norm():
                act.wait_ge(stats_full, stats.up())
                inverse_rms(rY[:, 0:SEQ], M[:, 0, :], r_ready, yr)

            def hi_of(dst, src, scale=1.0):
                nc.scalar.activation(dst, src, ACT.Copy, scale=scale).then_inc(mh_ready, 1)

            def transposed(dst, src):
                act.wait_ge(tr_full, trf.up())
                nc.scalar.copy(dst, src).then_inc(tr_done, 1)

            def mixer1():
                wait_evacuated(0)
                for t in range(4):
                    transposed(VT[:, t, :], M[:, t % 2, :])
                for t in range(2):
                    transposed(VR[:, 2 * t:2 * t + 2, :].rearrange("p a b -> p (a b)"), M[:, t, :])
                act.wait_ge(lam_full, olm.up())
                nc.scalar.activation(lam[:, 2:4], M[:, 2, 0:2], ACT.Exp, scale=float(D)).then_inc(lam_exp, 1)
                for m in range(2):
                    act.wait_ge(centred, cen.up())
                    nc.scalar.activation(sq[:, m, 0:SEQ], PR[:, 12 + m, :], ACT.Square).then_inc(osq_ready, 1)
                inverse_rms_pair([(RC[:, m, :], M[:, m, :]) for m in range(2)], rg_ready, rg)
                for m in range(2):
                    nc.scalar.activation(RS[:, m, :], PR[:, 16 + m, :], ACT.Tanh, scale=0.5).then_inc(silu_ready, 1)
                for m in range(2):
                    act.wait_ge(o_ready, orr.up())
                    hi_of(xh[:, 4 + m, 0:SEQ], PR[:, 12 + m, :], 0.5)
                for m in range(2):
                    act.wait_ge(pool_full, pf.up())
                    hi_of(xh[:, 6 + m, 0:SEQ], M[:, m, :], gain(C_PSC, m))

                def exps(u):
                    b, W = u % 2, (u % 4 + 1) * P
                    act.wait_ge(max_ready, mx.up())
                    for m in range(2):
                        ins = nc.scalar.activation(PB[:, b, m, 0:W], acc[b][:, m, 0:W], ACT.Exp, scale=0.125,
                                                   bias=MX[:, b, 2 + m:3 + m], accum_out=MX[:, b, 4 + m:5 + m])
                    ins.then_inc(exp_ready, 1)

                def copy_t(u):
                    b, W = u % 2, (u % 4 + 1) * P
                    act.wait_ge(at_full, atf.up())
                    act.wait_ge(av_done, av.up())
                    nc.scalar.copy(AT[:, b, 0:W], M[:, b, 0:W]).then_inc(at_ready, 1)

                exps(0)
                for u in range(16):
                    if u < 15:
                        exps(u + 1)
                    copy_t(u)
                for pair in range(2):
                    for h in (2 * pair, 2 * pair + 1):
                        act.wait_ge(o_evac, oe.up())
                        nc.scalar.activation(sq[:, h % 2, 0:SEQ], PR[:, 8 + h, :], ACT.Square).then_inc(osq_ready, 1)
                    inverse_rms_pair([(RC[:, h, :], M[:, h, :]) for h in range(2)], rg_ready, rg)
                    for h in (2 * pair, 2 * pair + 1):
                        act.wait_ge(o_ready, orr.up())
                        hi_of(xh[:, h, 0:SEQ], PR[:, 8 + h, :])
                act.wait_ge(ml_ready, mlr.up(8))

            def conv_up(m, half):
                dst = (G, V)[half]
                if half == 0:
                    split_hi()
                wait_evacuated()
                if half == 1:
                    act.wait_ge(ff_ready, ffr.now())
                    ffr.up()
                nc.scalar.activation(dst[:, 0:SEQ], U[:, 0:SEQ], ACT.Identity, scale=gain(C_CW + 2 * 2 * FT + half * FT, m),
                                     bias=gain(C_CB + half * FT, m)).then_inc(tap_ready, 1)
                if half == 1:
                    split_hi()
                if half == 0:
                    act.wait_ge(conv_done, conv.up())
                    nc.scalar.activation(G[:, 0:SEQ], G[:, 0:SEQ], ACT.Gelu_apprx_tanh).then_inc(gate_act, 1)
                else:
                    prod.up()

            def down(trips=4):
                with loop(act, trips, [(stg[0], 48), (stg[1], 48), (free, 6)]):
                    for _ in range(6):
                        split_hi()
                wait_evacuated(KT)

            def layer1():
                act.wait_ge(param_in, prm.up(32))
                norm_in(SEQ, C_PRE, False)
                with loop(act, IN1 // 2, [(stg[0], 16), (stg[1], 16), (free, 2)]):
                    split_hi()
                    split_hi()
                wait_evacuated(IN1)
                act.wait_ge(param_in, prm.up(16))
                mixer1()
                with loop(act, OUT1 // 2, [(stg[0], 16), (stg[1], 16), (free, 2)]):
                    split_hi()
                    split_hi()
                wait_evacuated(OUT1)
                post_norm()
                norm_in(SEQ, C_MPRE, True)
                with loop(act, FT, [(stg[0], 16), (stg[1], 16), (free, 2), (ev, 2), (conv, 1), (prod, 1),
                                    (steps, 1), (ffr, 1)]) as m:
                    choose_table(ACT.Gelu_apprx_tanh)
                    for half in range(2):
                        conv_up(m, half)
                down()
                post_norm()
                act.wait_ge(x_ready, xr.up(KT))

            def ffn2(gcol):
                norm_in(TALL, gcol, False)
                with loop(act, FT, [(stg[0], 16), (stg[1], 16), (free, 2), (ev, 2), (prod, 1), (steps, 1)]) as m:
                    choose_table(ACT.Silu)
                    split_hi()
                    wait_evacuated()
                    nc.scalar.activation(G[:, :], G[:, :], ACT.Silu).then_inc(gate_act, 1)
                    split_hi()
                    wait_evacuated()
                    act.wait_ge(prod_ready, prod.up())
                    nc.scalar.copy(tile_of(fh, m, TALL), U[:, :]).then_inc(fh_ready, 1)
                ffr.up(FT)
                down()

            def gated(T=TALL):
                for t, (c0, n) in enumerate(TILES2):
                    act.wait_ge(z_full, zf.up())
                    chain(nc.scalar.activation(LG[0:n, t, :], z_bank(t, n), ACT.Abs))
                    chain(nc.scalar.activation(LG[0:n, t, :], LG[0:n, t, :], ACT.Exp, scale=-1.0))
                for t, (c0, n) in enumerate(TILES2):
                    nc.scalar.activation(LG[0:n, t, :], LG[0:n, t, :], ACT.Ln, bias=one_c[0:n, :]).then_inc(lnz_ready, 1)
                for t, (c0, n) in enumerate(TILES2):
                    transposed(VA[0:n, t, :], M[0:n, 2 + t % 2, :])
                for dm in range(4):
                    act.wait_ge(cum_full, cumf.up())
                    act.wait_ge(e_used, eu.up())
                    for dst, s in ((E1, 1.0), (E2, -1.0)):
                        nc.scalar.activation(dst[:, 0:272], M[:, 2 * (dm % 2), 0:272], ACT.Exp, scale=s)
                        ins = nc.scalar.activation(dst[:, 272:TALL], M[:, 2 * (dm % 2) + 1, 0:256], ACT.Exp, scale=s)
                    ins.then_inc(e_ready, 1)
                for t, (c0, n) in enumerate(TILES2):
                    transposed(LG[0:n, t, :], M[0:n, t % 2, :])
                for pair in range(2):
                    for h in (2 * pair, 2 * pair + 1):
                        act.wait_ge(go_evac, goe.up())
                        nc.scalar.activation(sq[:, h % 2, :], PR2[:, h, :], ACT.Square).then_inc(osq_ready, 1)
                    inverse_rms_pair([(like(QD[:, h, :], T), view(M[:, 2 * h:2 * h + 2, :], T)) for h in range(2)],
                                     rg_ready, rg)
                    for h in (2 * pair, 2 * pair + 1):
                        nc.scalar.activation(KI[:, h % 2, :], PR2[:, 8 + h, :], ACT.Tanh, scale=0.5).then_inc(silu_ready, 1)
                    for h in (2 * pair, 2 * pair + 1):
                        act.wait_ge(o_ready, orr.up())
                        hi_of(mh[:, h, :], PR2[:, h, :], 0.5)

            def attention2(T=TALL):
                act.wait_ge(ml_ready, mlr.up(4))
                for tiles in ((0, 1), (2, 3), (4,)):
                    for j in tiles:
                        if j > 1:
                            act.wait_ge(qn_ready, qn.up())
                        nc.scalar.activation(sq[:, j % 2, :], PR2[:, 12 + j, :], ACT.Square).then_inc(osq_ready, 1)
                    inverse_rms_pair([(like(PB2[:, j % 2, :], T), view(M[:, 2 * (j % 2):2 * (j % 2) + 2, :], T))
                                      for j in tiles], rg_ready, rg)
                act.wait_ge(qn_ready, qn.up(2))
                act.wait_ge(tr_full, trf.up())
                nc.scalar.copy(VB[:, 1:5, :].rearrange("p a b -> p (a b)"), M[:, 0, :])
                nc.scalar.copy(VB[0:META, 0, :], M[0:META, 1, 0:P]).then_inc(tr_done, 1)

                def exps(u):
                    b, i, h = u % 2, u // 8, u % 8
                    act.wait_ge(max_ready, mx.up())
                    act.wait_ge(at_full, atf.up() - 2)
                    nc.scalar.activation(like(PB2[0:QB, b, :], T), view(acc[b], T, QB), ACT.Exp, scale=0.125,
                                         bias=MX2[0:QB, b, 1:2], accum_out=SU2[0:QB, i % 2, h:h + 1]).then_inc(exp_ready, 1)

                def hi(i):
                    act.wait_ge(ot_full, obt.up())
                    nc.scalar.copy(mh[:, 4:8, QB * i:QB * i + QB],
                                   M[:, 2 + i % 2, 0:4 * QB].rearrange("p (m q) -> p m q", m=4)).then_inc(mh_ready, 1)

                exps(0)
                for u in range(8 * NQB):
                    if u < 8 * NQB - 1:
                        exps(u + 1)
                    if u % 8 == 4 and u > 8:
                        hi(u // 8 - 1)
                hi(NQB - 1)

            def merge():
                ffr.up(KT)
                act.wait_ge(half_bias, hb.up())
                act.wait_ge(ml_ready, mlr.up(NQB))
                with loop(act, 4, [(stg[0], 48), (stg[1], 48), (free, 6), (ev, 6), (prod, 2)]) as i:
                    for a in range(2):
                        for g, buf in enumerate((G0, G1)):
                            split_hi()
                            wait_evacuated()
                            nc.scalar.activation(buf[:, :], buf[:, :], ACT.Tanh, scale=0.5,
                                                 bias=gain(G_BM + 8 * g + a, 2 * i)).then_inc(gate_act, 1)
                        split_hi()
                        wait_evacuated()
                        act.wait_ge(prod_ready, prod.up())
                        nc.scalar.activation(tile_of(yh, 2 * i + a, TALL), T0[:, :], ACT.Copy, scale=0.5).then_inc(fh_ready, 1)

            def layer2():
                act.wait_ge(param_in, prm.up(32))
                ffn2(G_N)
                norm_in(TALL, G_N + 8, False)
                with loop(act, IN2 // 2, [(stg[0], 16), (stg[1], 16), (free, 2)]):
                    split_hi()
                    split_hi()
                wait_evacuated(IN2)
                act.wait_ge(param_in, prm.up(16))
                gated()
                attention2()
                merge()
                with loop(act, KT // 2, [(stg[0], 16), (stg[1], 16), (free, 2)]):
                    split_hi()
                    split_hi()
                wait_evacuated(KT)
                ffn2(G_N + 16)

            goe, qn, mlr, hb, ffr = Tally(2), Tally(), Tally(), Tally(), Tally()
            act.wait_ge(consts_in, 1)
            split_hi()
            split_hi()
            act.wait_ge(x_in_sem, 48)
            run_layers(act, layer1, layer2, (stg[0], stg[1], free, data, ev, steps, stats, yr, xr, tap, conv, ga, prod,
                                             trf, cen, ovf, rg, mx, atf, av, oe, orr, olm, pf, cumf, eu, zf, obt,
                                             goe, qn, mlr, hb, prm, ffr))
            act.wait_ge(stats_full, stats.up())
            inverse_rms(like(rB[:, 0:TALL], TALL), view(M[:, 0:2, :], TALL), r_ready, yr)

        @block.vector
        def _(dve):
            hi, free, data, lo_n, ev = Tally(), Tally(), Tally(2), Tally(), Tally(2)
            xhr, xlr, sqr, ssn, rr, ysc, steps = Tally(), Tally(), Tally(), Tally(2), Tally(1), Tally(), Tally()
            tap, cdone, ga, prod, fhr, ffr = Tally(), Tally(), Tally(), Tally(), Tally(), Tally()
            rotf, cosr, roped_n, scf, stn, stu = Tally(), Tally(), Tally(2), Tally(), Tally(2), Tally()
            meanf, cen, osb, rg, sil, orr, mhr, mlr = Tally(), Tally(), Tally(), Tally(), Tally(), Tally(), Tally(), Tally()
            win, pol, lin, lexp, mx, ex, ar, av, oe, prm = (Tally(), Tally(), Tally(), Tally(), Tally(), Tally(2),
                                                         Tally(), Tally(2), Tally(2), Tally())
            lnz, lgr, er, eun, kvf, stt, attf, atn, atu, gof, goe, qn = (Tally(), Tally(2), Tally(), Tally(1), Tally(), Tally(),
                                                                  Tally(), Tally(2), Tally(), Tally(), Tally(2), Tally())
            atf, atr, av2, obr, hb, outn, ldn, scd = Tally(2), Tally(2), Tally(), Tally(), Tally(), Tally(), Tally(), Tally()
            strip, slot = [0], [0]

            def link(ins, sem_, tally):
                ins.then_inc(sem_, 1)
                dve.wait_ge(sem_, tally.up())

            def chain(ins):
                link(ins, dve_step, steps)

            def split_lo():
                p = strip[0] % 2
                strip[0] += 1
                dve.wait_ge(hi_ready, hi.up())
                dve.wait_ge(strip_done, free.up())
                nc.vector.tensor_tensor(wlo[p][:, :], stage[p][:, :], whi[p][:, :].bitcast(F32),
                                        ALU.subtract).then_inc(lo_ready, 1)

            def wait_accumulated(strips=1):
                dve.wait_ge(strip_done, data.up(strips))
                slot[0] += 1
                return acc[(slot[0] - 1) % 2]

            def evacuate(dst, T):
                a = wait_accumulated()
                link(nc.vector.tensor_tensor(like(dst, T), view(a, T), like(rB[:, 0:T], T), ALU.mult), evacuated, ev)

            def wait_r():
                dve.wait_ge(r_ready, rr.up())

            def add_squares(m, T):
                dve.wait_ge(sq_ready, sqr.up())
                if m == 0:
                    ins = nc.vector.tensor_copy(ss[:, 0:T], sq[:, 0, 0:T])
                else:
                    ins = nc.vector.tensor_tensor(ss[:, 0:T], ss[:, 0:T], sq[:, m % 2, 0:T], ALU.add)
                link(ins, ss_added, ssn)

            def norm_in(T, gcol):
                for m in range(KT):
                    dve.wait_ge(xh_ready, xhr.up())
                    link(nc.vector.scalar_tensor_tensor(xl[:, m, 0:T], xs(m, T), gain(gcol, m), xh[:, m, 0:T].bitcast(F32),
                                                        ALU.mult, ALU.subtract), xl_ready, xlr)
                    add_squares(m, T)
                wait_r()

            def post_update(Y, gcol):
                wait_r()
                for m in range(KT):
                    link(nc.vector.scalar_tensor_tensor(Y[:, m, 0:SEQ], Y[:, m, 0:SEQ], gain(gcol, m), rY[:, 0:SEQ],
                                                        ALU.mult, ALU.mult), y_scaled, ysc)

            def lo_of(dst, src, part, scale=None):
                dve.wait_ge(mh_ready, mhr.up())
                if scale is None:
                    ins = nc.vector.tensor_tensor(dst, src, part, ALU.subtract)
                else:
                    ins = nc.vector.scalar_tensor_tensor(dst, src, scale, part, ALU.mult, ALU.subtract)
                link(ins, ml_ready, mlr)

            def mixer1():
                for a in range(2):
                    link(nc.vector.tensor_tensor(lam[:, a:a + 1], gain(C_LAM + 2 * a), gain(C_LAM + 2 * a + 1), ALU.mult),
                         lam_in, lin)
                chain(nc.vector.tensor_tensor(lam[:, 5:6], gain(C_SUB), gain(C_LINIT + 1), ALU.mult))
                dve.wait_ge(lam_exp, lexp.up())
                chain(nc.vector.tensor_tensor(lam[:, 4:5], lam[:, 3:4], lam[:, 2:3], ALU.subtract))
                chain(nc.vector.tensor_tensor(lam[:, 4:5], lam[:, 4:5], gain(C_LINIT), ALU.subtract))
                for j in range(10):
                    tile, tab = (j, 0) if j < 8 else (j + 4, 2)
                    dve.wait_ge(rot_full, rotf.up())
                    chain(nc.vector.tensor_tensor(RS[:, j % 2, :], M[:, 2 + j % 2, :],
                                                  tb1[:, (tab + 1) * SEQ:(tab + 2) * SEQ], ALU.mult))
                    dve.wait_ge(cos_ready, cosr.up())
                    link(nc.vector.tensor_tensor(PR[:, tile, :], RC[:, j % 2, :], RS[:, j % 2, :], ALU.add), roped, roped_n)
                for j in range(16):
                    h, jb = j // 4, j % 4
                    W = SEQ - jb * P
                    dve.wait_ge(sc_full, scf.up())
                    dve.wait_ge(st_used, stu.up())
                    link(nc.vector.tensor_tensor(AT[:, j % 2, 0:W], M[:, j % 2, 0:W],
                                                 tb1[:, (4 + h) * SEQ:(4 + h) * SEQ + W], ALU.mult), st_ready, stn)
                dve.wait_ge(st_used, stu.now() + 2)
                for m in range(2):
                    link(nc.vector.tensor_copy(PR[:, 12 + m, :], M[:, 2 + m, :]), o_sb, osb)
                for m in range(2):
                    dve.wait_ge(mean_full, meanf.up())
                    link(nc.vector.tensor_tensor(PR[:, 12 + m, :], PR[:, 12 + m, :], M[:, m, :], ALU.subtract), centred, cen)
                for m in range(2):
                    o = PR[:, 12 + m, :]
                    dve.wait_ge(rg_ready, rg.up())
                    chain(nc.vector.scalar_tensor_tensor(o, o, gain(C_RETG, m), RC[:, m, :], ALU.mult, ALU.mult))
                    dve.wait_ge(silu_ready, sil.up())
                    chain(nc.vector.scalar_tensor_tensor(RS[:, m, :], RS[:, m, :], 1.0, PR[:, 16 + m, :], ALU.add, ALU.mult))
                    link(nc.vector.tensor_tensor(o, o, RS[:, m, :], ALU.mult), o_ready, orr)
                for m in range(2):
                    lo_of(xl[:, 4 + m, 0:SEQ], PR[:, 12 + m, :], xh[:, 4 + m, 0:SEQ].bitcast(F32), 0.5)
                for m in range(2):
                    dve.wait_ge(win_ready, win.up())
                    s = WS[:, m, 1, :]
                    chain(nc.vector.tensor_tensor(s[:, 0:16], s[:, 0:16], con[:, K_REC + 16 * m:K_REC + 16 * m + 16], ALU.mult))
                    chain(nc.vector.tensor_scalar(s[:, 16:SEQ], s[:, 16:SEQ], con[:, K_REC + 32 + m:K_REC + 33 + m], None, ALU.mult))
                    link(nc.vector.tensor_tensor(WS[:, m, 0, :], s, PR[:, 18 + m, :], ALU.subtract), pooled, pol)
                for m in range(2):
                    lo_of(xl[:, 6 + m, 0:SEQ], M[:, m, :], xh[:, 6 + m, 0:SEQ].bitcast(F32), gain(C_PSC, m))

                def maxima(u):
                    b, W = u % 2, (u % 4 + 1) * P
                    dve.wait_ge(sc_full, scf.up())
                    diag = acc[b][:, :, W - P:W]
                    chain(nc.vector.tensor_tensor(diag, diag, con[:, K_CAUS:K_CAUS + 256].rearrange("p (m k) -> p m k", m=2),
                                                  ALU.add))
                    chain(nc.vector.reduce_max(MX[:, b, 0:2], acc[b][:, :, 0:W], AX_X))
                    link(nc.vector.tensor_scalar(MX[:, b, 2:4], MX[:, b, 0:2], -0.125, None, ALU.mult), max_ready, mx)

                def combine(u):
                    b, W = u % 2, (u % 4 + 1) * P
                    dve.wait_ge(exp_ready, ex.up())
                    chain(nc.vector.reciprocal(MX[:, b, 6:8], MX[:, b, 4:6]))
                    chain(nc.vector.tensor_tensor(MX[:, b, 7:8], MX[:, b, 7:8], lam[:, 4:5], ALU.mult))
                    chain(nc.vector.tensor_scalar(PB[:, b, 1, 0:W], PB[:, b, 1, 0:W], MX[:, b, 7:8], None, ALU.mult))
                    link(nc.vector.scalar_tensor_tensor(PB[:, b, 0, 0:W], PB[:, b, 0, 0:W], MX[:, b, 6:7], PB[:, b, 1, 0:W],
                                                        ALU.mult, ALU.add), a_ready, ar)

                def evac_head(h):
                    dve.wait_ge(av_done, av.up(4))
                    link(nc.vector.tensor_copy(PR[:, 8 + h, :], M[:, 2 + h % 2, :]), o_evac, oe)

                maxima(0)
                for u in range(16):
                    if u < 15:
                        maxima(u + 1)
                    combine(u)
                    if u % 4 == 1 and u > 4:
                        evac_head(u // 4 - 1)
                evac_head(3)
                atf.up(16)
                atr.up(16)
                av2.up(16)
                for pair in range(2):
                    for h in (2 * pair, 2 * pair + 1):
                        dve.wait_ge(rg_ready, rg.up())
                        link(nc.vector.scalar_tensor_tensor(PR[:, 8 + h, :], PR[:, 8 + h, :], lam[:, 5:6], RC[:, h % 2, :],
                                                            ALU.mult, ALU.mult), o_ready, orr)
                    for h in (2 * pair, 2 * pair + 1):
                        lo_of(xl[:, h, 0:SEQ], PR[:, 8 + h, :], xh[:, h, 0:SEQ].bitcast(F32))

            def store_y(Y, m, strips, between, T=SEQ):
                a = wait_accumulated(strips)
                link(nc.vector.tensor_copy(tile_of(Y, m, SEQ), a[:, 0, :]), evacuated, ev)
                between()
                dve.wait_ge(sq_ready, sqr.up())
                return a

            def y_squares(b):
                link(nc.vector.tensor_tensor(ss[:, 0:SEQ], ss[:, 0:SEQ], sq[:, b, 0:SEQ], ALU.add), ss_added, ssn)

            def conv_up(m, half):
                dst = (G, V)[half]
                a = wait_accumulated()
                link(nc.vector.tensor_tensor(U[:, 0:SEQ], a[:, 0, :], rB[:, 0:SEQ], ALU.mult), evacuated, ev)
                if half == 0:
                    split_lo()
                dve.wait_ge(tap_ready, tap.up())
                for back in (1, 2):
                    w = gain(C_CW + (2 - back) * 2 * FT + half * FT, m)
                    ins = nc.vector.scalar_tensor_tensor(dst[:, back:SEQ], U[:, 0:SEQ - back], w, dst[:, back:SEQ],
                                                         ALU.mult, ALU.add)
                    if back == 1:
                        chain(ins)
                        if half == 1:
                            split_lo()
                    elif half == 0:
                        link(ins, conv_done, cdone)
                    else:
                        chain(ins)
                if half == 1:
                    dve.wait_ge(gate_act, ga.up())
                    link(nc.vector.tensor_tensor(V[:, 0:SEQ], V[:, 0:SEQ], G[:, 0:SEQ], ALU.mult), prod_ready, prod)
                    fhr.up()
                    ffr.up()

            def layer1():
                dve.wait_ge(param_in, prm.up(32))
                norm_in(SEQ, C_PRE)
                with loop(dve, IN1 // 2, [(hi, 2), (free, 2), (data, 2), (ev, 2)]) as i:
                    for a in range(2):
                        evacuate(tile_of(PR, 2 * i + a, SEQ), SEQ)
                        split_lo()
                dve.wait_ge(param_in, prm.up(16))
                mixer1()
                chain(nc.vector.memset(ss[:, 0:SEQ], 0.0))
                with loop(dve, OUT1 // 2, [(hi, 2), (free, 2), (data, 2), (ev, 2), (sqr, 2), (ssn, 2)]) as i:
                    for a in range(2):
                        store_y(PR, 2 * i + a, 1, split_lo)
                        y_squares(a)
                post_update(PR, C_POST)
                norm_in(SEQ, C_MPRE)
                with loop(dve, FT, [(hi, 2), (free, 2), (data, 2), (ev, 2), (tap, 2), (cdone, 1), (ga, 1), (prod, 1),
                                    (fhr, 1), (ffr, 1), (steps, 3)]) as m:
                    for half in range(2):
                        conv_up(m, half)
                chain(nc.vector.memset(ss[:, 0:SEQ], 0.0))
                with loop(dve, 4, [(hi, 6), (free, 6), (data, 6), (ev, 2), (sqr, 2), (ssn, 2)]) as i:
                    for a in range(2):
                        split_lo()
                        split_lo()
                        store_y(Yf, 2 * i + a, 3, split_lo)
                        y_squares(a)
                post_update(Yf, C_MPOST)
                dve.sem_inc(layer_done, 1)

            def down2():
                with loop(dve, 4, [(hi, 6), (free, 6), (data, 6), (ev, 2)]) as i:
                    for a in range(2):
                        split_lo()
                        split_lo()
                        s = wait_accumulated(3)
                        xm = like(xs(2 * i + a, TALL), TALL)
                        link(nc.vector.scalar_tensor_tensor(xm, view(s, TALL), 0.5, xm, ALU.mult, ALU.add), evacuated, ev)
                        split_lo()

            def ffn2(gcol):
                norm_in(TALL, gcol)
                with loop(dve, FT, [(hi, 2), (free, 2), (data, 2), (ev, 2), (ga, 1), (prod, 1), (fhr, 1), (ffr, 1)]) as m:
                    evacuate(G[:, :], TALL)
                    split_lo()
                    evacuate(U[:, :], TALL)
                    dve.wait_ge(gate_act, ga.up())
                    link(nc.vector.tensor_tensor(U[:, :], U[:, :], G[:, :], ALU.mult), prod_ready, prod)
                    split_lo()
                    dve.wait_ge(fh_ready, fhr.up())
                    link(nc.vector.tensor_tensor(tile_of(fl, m, TALL), U[:, :], tile_of(fh, m, TALL).bitcast(F32),
                                                 ALU.subtract), ff_ready, ffr)
                down2()

            def gated():
                for t, (c0, n) in enumerate(TILES2):
                    dve.wait_ge(lnz_ready, lnz.up())
                    link(nc.vector.scalar_tensor_tensor(LG[0:n, t, :], z_bank(t, n), 0.0, LG[0:n, t, :],
                                                        ALU.min, ALU.subtract), lg_ready, lgr)
                for dm in range(4):
                    mt = dm % 2
                    dve.wait_ge(e_ready, er.up())
                    chain(nc.vector.scalar_tensor_tensor(QD[:, dm, :], PR2[:, mt, :], 0.125, E1[:, :], ALU.mult, ALU.mult))
                    chain(nc.vector.tensor_tensor(KI[:, dm, :], PR2[:, 2 + mt, :], E2[:, :], ALU.mult))
                    first, rest = (META - 1, META + 63) if dm < 2 else (0, META)
                    chain(nc.vector.tensor_copy(DC[:, dm, 0:1], E1[:, first:first + 1]))
                    link(nc.vector.tensor_copy(DC[:, dm, 1:9], E1[:, rest:rest + 7 * 64 + 1:64]), e_used, eun)
                for mt in range(2):
                    for d in range(2):
                        dm = 2 * d + mt
                        s = lambda c, k=1: SS[:, d, c * P:(c + k) * P]
                        dve.wait_ge(kv_full, kvf.up())
                        for g in range(2):
                            dec = DC[:, dm, d + 4 * g:d + 4 * g + 4].unsqueeze(2).to_broadcast([P, 4, P])
                            chain(nc.vector.tensor_tensor(s(4 * g, 4).rearrange("p (c v) -> p c v", c=4),
                                                          M[:, 2 * d + g, :].rearrange("p (c v) -> p c v", c=4), dec, ALU.mult))
                        for c in (range(1, 8) if d == 0 else range(6, -1, -1)):
                            prev = c - 1 if d == 0 else c + 1
                            ins = nc.vector.scalar_tensor_tensor(s(c), s(prev), DC[:, dm, c + d:c + d + 1], s(c),
                                                                 ALU.mult, ALU.add)
                            if c == (7, 0)[d]:
                                link(ins, state_ready, stt)
                            else:
                                chain(ins)
                    for t, (c0, n) in enumerate(TILES2):
                        dve.wait_ge(att_full, attf.up())
                        dve.wait_ge(att_used, atu.up())
                        four = lambda a: a.rearrange("p (h d k) -> p h d k", h=2, d=2)[0:n, :, :, 0:n]
                        ps = M[0:n, 2 * (t % 2):2 * (t % 2) + 2, 0:256].rearrange("p h (d k) -> p h d k", d=2)[:, :, :, 0:n]
                        link(nc.vector.tensor_tensor(four(ATG[:, t % 2, :]), ps, four(tb2[:, 2 * TALL:]),
                                                     ALU.mult), att_ready, atn)
                    dve.wait_ge(go_full, gof.up())
                    for h in range(2):
                        chain(nc.vector.tensor_copy(PR2[:, 2 * mt + h, 0:272], acc[h][:, 0, 0:272]))
                        link(nc.vector.tensor_copy(PR2[:, 2 * mt + h, 272:TALL], acc[h][:, 1, 0:256]), go_evac, goe)
                for pair in range(2):
                    for h in (2 * pair, 2 * pair + 1):
                        o, th = PR2[:, h, :], KI[:, h % 2, :]
                        dve.wait_ge(rg_ready, rg.up())
                        chain(nc.vector.scalar_tensor_tensor(o, o, gain(G_GN, h), QD[:, h % 2, :], ALU.mult, ALU.mult))
                        dve.wait_ge(silu_ready, sil.up())
                        chain(nc.vector.scalar_tensor_tensor(th, th, 1.0, PR2[:, 8 + h, :], ALU.add, ALU.mult))
                        link(nc.vector.tensor_tensor(o, o, th, ALU.mult), o_ready, orr)
                    for h in (2 * pair, 2 * pair + 1):
                        lo_of(ml[:, h, :], PR2[:, h, :], mh[:, h, :].bitcast(F32), 0.5)

            def attention2(T=TALL):
                cos, sin = tb2[:, 0:T], tb2[:, T:2 * T]
                for j in range(5):
                    dve.wait_ge(rg_ready, rg.up())
                    link(nc.vector.scalar_tensor_tensor(PR2[:, 12 + j, :], PR2[:, 12 + j, :], gain(G_QN if j < 4 else G_KN),
                                                        PB2[:, j % 2, :], ALU.mult, ALU.mult), qn_ready, qn)
                for j in range(4):
                    q, ps = PR2[:, 12 + j, :], M[:, 2 * (j % 2):2 * (j % 2) + 2, :]
                    dve.wait_ge(rot_full, rotf.up())
                    chain(nc.vector.tensor_tensor(like(PB2[:, 0, :], T), view(ps, T), like(sin, T), ALU.mult))
                    chain(nc.vector.tensor_tensor(q, q, cos, ALU.mult))
                    link(nc.vector.tensor_tensor(q, q, PB2[:, 0, :], ALU.add), roped, roped_n)
                for kv in range(2):
                    dve.wait_ge(rot_full, rotf.up())
                    chain(nc.vector.tensor_tensor(like(PB2[:, 0, :], T), view(M[:, 0:2, :], T), like(cos, T), ALU.mult))
                    chain(nc.vector.tensor_tensor(like(PB2[:, 1, :], T), view(M[:, 2:4, :], T), like(sin, T), ALU.mult))
                    link(nc.vector.tensor_tensor(K2[:, kv, :], PB2[:, 0, :], PB2[:, 1, :], ALU.add), roped, roped_n)

                def maxima(u):
                    b = u % 2
                    dve.wait_ge(sc_full, scf.up())
                    chain(nc.vector.tensor_reduce(MX2[0:QB, b, 0:1], view(acc[b], T, QB), mybir.AxisListType.XY, ALU.max))
                    link(nc.vector.tensor_scalar(MX2[0:QB, b, 1:2], MX2[0:QB, b, 0:1], -0.125, None, ALU.mult), max_ready, mx)

                def copy_t(u):
                    b = u % 2
                    dve.wait_ge(at_full, atf.up())
                    dve.wait_ge(av_done, av2.up())
                    src = M[:, b, 0:5 * QB].rearrange("p (t q) -> p t q", t=5)
                    chain(nc.vector.tensor_copy(PT2[:, b, 1:5, :], src[:, 1:5, :]))
                    link(nc.vector.tensor_copy(PT2[0:META, b, 0, :], src[0:META, 0, :]), at_ready, atr)

                def out_tokens(i):
                    b = i % 2
                    dve.wait_ge(av_done, av.up(8))
                    chain(nc.vector.reciprocal(RI2[0:QB, b, :], SU2[0:QB, b, :]))
                    link(nc.vector.tensor_tensor(OB[0:QB, b, :].rearrange("p (h v) -> p h v", h=8),
                                                 M[0:QB, 2 + b, :].rearrange("p (h v) -> p h v", h=8),
                                                 RI2[0:QB, b, :].unsqueeze(2).to_broadcast([QB, 8, 64]), ALU.mult), ob_ready, obr)

                def lo(i):
                    c = slice(QB * i, QB * i + QB)
                    lo_of(ml[:, 4:8, c], M[:, 2 + i % 2, 0:4 * QB].rearrange("p (m q) -> p m q", m=4),
                          mh[:, 4:8, c].bitcast(F32))

                maxima(0)
                for u in range(8 * NQB):
                    if u < 8 * NQB - 1:
                        maxima(u + 1)
                    copy_t(u)
                    if u > 8 and u % 8 == 2:
                        out_tokens(u // 8 - 1)
                    if u > 8 and u % 8 == 5:
                        lo(u // 8 - 1)
                out_tokens(NQB - 1)
                lo(NQB - 1)

            def merge():
                link(nc.vector.tensor_scalar(par[:, G_BM:G_BM + 16], par[:, G_BM:G_BM + 16], 0.5, None, ALU.mult), half_bias, hb)
                with loop(dve, 4, [(hi, 6), (free, 6), (data, 6), (ev, 6), (ga, 4), (prod, 2), (fhr, 2), (ffr, 2),
                                   (steps, 2)]) as i:
                    for a in range(2):
                        for g, buf in enumerate((G0, G1)):
                            evacuate(buf[:, :], TALL)
                            split_lo()
                        s = wait_accumulated()
                        dve.wait_ge(gate_act, ga.up(2))
                        chain(nc.vector.scalar_tensor_tensor(like(G1[:, :], TALL), like(G1[:, :], TALL), 1.0,
                                                             view(M[:, 2:4, :], TALL), ALU.add, ALU.mult))
                        link(nc.vector.scalar_tensor_tensor(like(G0[:, :], TALL), like(G0[:, :], TALL), 1.0,
                                                            view(s, TALL), ALU.add, ALU.mult), evacuated, ev)
                        link(nc.vector.tensor_tensor(T0[:, :], G0[:, :], G1[:, :], ALU.add), prod_ready, prod)
                        split_lo()
                        dve.wait_ge(fh_ready, fhr.up())
                        link(nc.vector.scalar_tensor_tensor(tile_of(yl, 2 * i + a, TALL), T0[:, :], 0.5,
                                                            tile_of(yh, 2 * i + a, TALL).bitcast(F32), ALU.mult, ALU.subtract),
                             ff_ready, ffr)

            def layer2():
                dve.wait_ge(param_in, prm.up(32))
                ffn2(G_N)
                norm_in(TALL, G_N + 8)
                with loop(dve, 6, [(hi, 2), (free, 2), (data, 2), (ev, 2)]) as i:
                    for a in range(2):
                        evacuate(tile_of(PR2, 2 * i + a, TALL), TALL)
                        split_lo()
                chain(nc.vector.memset(LR[32:64, :], 1.0))
                s = wait_accumulated()
                link(nc.vector.tensor_tensor(like(LR[0:32, :], TALL), view(s, TALL, 32), like(rB[0:32, :], TALL), ALU.mult),
                     evacuated, ev)
                split_lo()
                for m in range(12, 18):
                    evacuate(PR2[:, m, :], TALL)
                    split_lo()
                wait_accumulated()
                dve.sem_inc(evacuated, 1)
                ev.up()
                split_lo()
                dve.wait_ge(param_in, prm.up(16))
                gated()
                attention2()
                merge()
                with loop(dve, KT // 2, [(hi, 2), (free, 2), (data, 2), (ev, 2)]) as i:
                    for a in range(2):
                        s = wait_accumulated()
                        xm = like(xs(2 * i + a, TALL), TALL)
                        link(nc.vector.tensor_tensor(xm, view(s, TALL), xm, ALU.add), evacuated, ev)
                        split_lo()
                ffn2(G_N + 16)
                dve.sem_inc(layer_done, 1)

            dve.wait_ge(consts_in, 1)
            split_lo()
            split_lo()
            dve.wait_ge(x_in_sem, 48)
            run_layers(dve, layer1, layer2, (hi, free, data, lo_n, ev, xhr, xlr, sqr, ssn, rr, ysc, steps, tap, cdone, ga,
                                             prod, fhr, ffr, rotf, cosr, roped_n, scf, stn, stu, meanf, cen, osb, rg, sil,
                                             orr, mhr, mlr, win, pol, lin, lexp, mx, ex, ar, av, oe, prm, lnz, lgr, er, eun,
                                             kvf, stt, attf, atn, atu, gof, goe, qn, atf, atr, av2, obr, hb))
            for m in range(KT):
                add_squares(m, TALL)
            wait_r()
            for m in range(KT):
                nc.vector.scalar_tensor_tensor(x[:, m, :], x[:, m, :], fng[:, m:m + 1], rB[:, :],
                                               ALU.mult, ALU.mult).then_inc(out_ready, 1)

        @block.gpsimd
        def _(pool):
            prod, fhr, ffr = Tally(), Tally(), Tally()
            ev, ssn, sqr, ysc, xr, prm, ldn, cosn, rop, wn, steps = (Tally(2), Tally(), Tally(), Tally(), Tally(), Tally(),
                                                                  Tally(), Tally(), Tally(), Tally(), Tally())

            def link(ins, sem_, tally):
                ins.then_inc(sem_, 1)
                pool.wait_ge(sem_, tally.up())

            def load(dst, src):
                settle(pool)
                pool.dma_start(dst, src).then_inc(param_in, 16)

            def square(m, src, T):
                pool.wait_ge(ss_added, ssn.up())
                nc.gpsimd.tensor_tensor(sq[:, m % 2, 0:T], src, src, ALU.mult).then_inc(sq_ready, 1)

            def norm_in(T, Y=None):
                for m in range(KT):
                    if Y is not None:
                        add_update(m, Y)
                    square(m, xs(m, T), T)

            def add_update(m, Y):
                pool.wait_ge(y_scaled, ysc.up())
                link(nc.gpsimd.tensor_tensor(xs(m, SEQ), xs(m, SEQ), Y[:, m, 0:SEQ], ALU.add), x_ready, xr)

            def y_squares(Y, trips):
                with loop(pool, KT // 2, [(ev, 2), (ssn, 2)]) as i:
                    for a in range(2):
                        pool.wait_ge(evacuated, ev.up())
                        square(a, tile_of(Y, 2 * i + a, SEQ), SEQ)

            def windows():
                plan = [[(1, 0, P, -1, 0), (2, 64, P, 0, 1), (0, 0, 64, 0, 1)],
                        [(1, 0, P, -1, 0), (2, 0, P, 0, 1), (4, 0, P, 1, 0), (8, 64, P, 0, 1), (0, 0, 64, 0, 1)]]
                for m in range(2):
                    for k, (back, lo, up, frm, to) in enumerate(plan[m]):
                        src = PR[lo:up, 18 + m, :] if frm < 0 else WS[lo:up, m, frm, :]
                        dst = WS[lo:up, m, to, :]
                        if back:
                            link(nc.gpsimd.tensor_tensor(dst[:, back:SEQ], src[:, back:SEQ], src[:, 0:SEQ - back], ALU.add),
                                 pool_step, steps)
                        settle(pool)
                        ins = nc.gpsimd.tensor_copy(dst[:, 0:back or SEQ], src[:, 0:back or SEQ])
                        if k == len(plan[m]) - 1:
                            link(ins, win_ready, wn)
                        else:
                            link(ins, pool_step, steps)

            def layer1():
                pool.wait_ge(layer_done, ldn.up())
                load(par[:, 0:NP1], params1[now_layer[0]])
                load(con[:, 0:NC2], consts1)
                norm_in(SEQ)
                pool.wait_ge(param_in, prm.up(32))
                load(tb1[:, :], tables1)
                pool.wait_ge(evacuated, ev.up(IN1))
                pool.wait_ge(param_in, prm.up(16))
                for j in range(10):
                    tile, tab = (j, 0) if j < 8 else (j + 4, 2)
                    pool.wait_ge(roped, rop.up())
                    nc.gpsimd.tensor_tensor(RC[:, j % 2, :], PR[:, tile, :], tb1[:, tab * SEQ:(tab + 1) * SEQ],
                                            ALU.mult).then_inc(cos_ready, 1)
                windows()
                y_squares(PR, OUT1)
                norm_in(SEQ, PR)
                with loop(pool, FT, [(prod, 1), (fhr, 1), (ffr, 1)]) as m:
                    pool.wait_ge(prod_ready, prod.up())
                    settle(pool)
                    link(nc.gpsimd.tensor_copy(tile_of(fh, m, SEQ), V[:, 0:SEQ]), fh_ready, fhr)
                    link(nc.gpsimd.tensor_tensor(tile_of(fl, m, SEQ), V[:, 0:SEQ], tile_of(fh, m, SEQ).bitcast(F32),
                                                 ALU.subtract), ff_ready, ffr)
                pool.wait_ge(evacuated, ev.up(2 * FT))
                y_squares(Yf, KT)
                for m in range(KT):
                    add_update(m, Yf)

            def layer2():
                prod.up(2 * FT + KT)
                fhr.up(2 * FT + KT)
                ffr.up(2 * FT + KT)
                pool.wait_ge(layer_done, ldn.up())
                load(par[:, 0:NP2], params2[now_layer[0]])
                load(con[:, 0:NC2], consts2)
                norm_in(TALL)
                pool.wait_ge(evacuated, ev.up(2 * FT + KT))
                load(tb2[:, :], tables2)
                norm_in(TALL)
                pool.wait_ge(roped, rop.up(6))
                pool.wait_ge(evacuated, ev.up(IN2 + 3 * KT + KT))
                pool.wait_ge(param_in, prm.up(48))
                norm_in(TALL)
                pool.wait_ge(evacuated, ev.up(2 * FT + KT))

            nc.gpsimd.memset(eps_one[:, 0:1], EPS)
            nc.gpsimd.memset(eps_one[:, 1:2], 1.0).then_inc(consts_in, 1)
            for s, k in ((strip_done, 2), (evacuated, 2), (ss_added, 2), (r_ready, 1), (layer_done, 1), (tr_done, 2),
                         (roped, 2), (st_ready, 2), (st_used, 2), (exp_ready, 2), (at_ready, 2), (av_done, 2),
                         (o_evac, 2), (lg_ready, 2), (e_used, 1), (att_ready, 2), (att_used, 2), (go_evac, 2),
                         (at_full, 2)):
                pool.sem_inc(s, k)
            pool.wait_ge(x_in_sem, 48)
            run_layers(pool, layer1, layer2, (ev, ssn, sqr, ysc, xr, prm, ldn, cosn, rop, wn, steps, prod, fhr, ffr))
            norm_in(TALL)

        @block.tensor
        def _(pe):
            hi, lo, ev, ssn, rr, xhr, xlr, ffr, mlr = (Tally(), Tally(), Tally(), Tally(2), Tally(), Tally(), Tally(), Tally(),
                                                      Tally())
            trd, lin, lexp, rop, stf, std, osb, osq, rg, pol = (Tally(), Tally(), Tally(), Tally(), Tally(), Tally(2), Tally(),
                                                            Tally(), Tally(), Tally())
            exf, ar, atf, atd, oef, lgr, eu, kvn, stt, atnf, atnd, gev, cen = (
                Tally(), Tally(), Tally(), Tally(2), Tally(), Tally(), Tally(), Tally(), Tally(), Tally(), Tally(2), Tally(),
                Tally())
            qn, exd, obr, prm, pes = Tally(), Tally(2), Tally(), Tally(), Tally()
            strip, slot = [0], [0]
            ident, ones = con[:, K_ID:K_ID + P], con[:, K_ONES:K_ONES + P]
            ones128, blk = con[:, K_ONE128:K_ONE128 + P], con[:, K_BLK:K_BLK + P]
            mm = nc.tensor.matmul

            def multiply(parts, start=True, stop=True, per_tile=None):
                p = strip[0] % 2
                strip[0] += 1
                pe.wait_ge(hi_ready, hi.up())
                pe.wait_ge(lo_ready, lo.up())
                for tiles, ps, T in parts:
                    last = len(tiles) - 1
                    for n, (k, fh_, fl_, kt) in enumerate(tiles):
                        w, v = whi[p][:, k * P:(k + 1) * P], wlo[p][:, k * P:(k + 1) * P]
                        hs = halves(T)
                        if per_tile:
                            per_tile()
                        for q, (ww, act_) in enumerate(((w, fh_), (w, fl_), (v, fh_))):
                            for b, t0, tn in hs:
                                ins = mm(ps[:, b, 0:tn], ww, act_[:, kt, t0:t0 + tn],
                                         start=start and n == 0 and q == 0, stop=stop and n == last and q == 2)
                ins.then_inc(strip_done, 1)

            def next_slot():
                pe.wait_ge(evacuated, ev.up())
                slot[0] += 1
                return acc[(slot[0] - 1) % 2]

            def project(T, h=None, l=None):
                h, l = h or xh, l or xl
                multiply([([(k, h, l, k) for k in range(KT)], next_slot(), T)])

            def first_pair(T):
                multiply([([(k, xh, xl, k) for k in range(KT)], next_slot(), T)],
                         per_tile=lambda: pe.wait_ge(xl_ready, xlr.up()))
                stats(T)
                project(T)

            def all_evacuated():
                pe.wait_ge(evacuated, ev.now() + 2)

            def down(T):
                with loop(pe, 4, [(hi, 6), (lo, 6), (ev, 2)]):
                    for a in range(2):
                        s = next_slot()
                        for j in range(3):
                            n = min(KT, FT - KT * j)
                            multiply([([(k, fh, fl, KT * j + k) for k in range(n)], s, T)], j == 0, j == 2)

            def stats(T):
                pe.wait_ge(ss_added, ssn.up(KT))
                pe.wait_ge(r_ready, rr.up())
                for b, t0, tn in halves(T):
                    ins = mm(M[:, b, 0:tn], ones, ss[:, t0:t0 + tn], start=True, stop=True)
                ins.then_inc(stats_full, 1)

            def rows(bank, a, b):
                for n, t0, tn in halves(b.shape[-1]):
                    ins = mm(bank[:, n, 0:tn], a, b[:, t0:t0 + tn], start=True, stop=True)
                return ins

            def mixer1():
                all_evacuated()
                for j in range(4):
                    pe.wait_ge(tr_done, trd.up())
                    for h in range(4):
                        ins = nc.tensor.transpose(M[:, j % 2, h * P:(h + 1) * P], PR[:, 8 + h, j * P:(j + 1) * P], ident)
                    ins.then_inc(tr_full, 1)
                for j in range(2):
                    pe.wait_ge(tr_done, trd.up())
                    for t in range(2):
                        for m in range(2):
                            c = (2 * j + t) * P
                            ins = nc.tensor.transpose(M[:, j, t * 256 + m * P:t * 256 + (m + 1) * P],
                                                      PR[:, 14 + m, c:c + P], ident)
                    ins.then_inc(tr_full, 1)
                pe.wait_ge(lam_in, lin.up(2))
                mm(M[:, 2, 0:2], ones, lam[:, 0:2], start=True, stop=True).then_inc(lam_full, 1)
                pe.wait_ge(lam_exp, lexp.up())
                for j in range(10):
                    tile, perm = (j, K_PDA) if j < 8 else (j + 4, K_PR)
                    pe.wait_ge(roped, rop.up())
                    mm(M[:, 2 + j % 2, :], con[:, perm:perm + P], PR[:, tile, :], start=True, stop=True).then_inc(rot_full, 1)
                pe.wait_ge(roped, rop.now() + 2)
                pe.wait_ge(tr_done, trd.now() + 2)

                def ret_scores(j):
                    h, jb = j // 4, j % 4
                    r = slice(32 * h, 32 * h + 32)
                    pe.wait_ge(st_ready, stf.up())
                    mm(M[:, j % 2, 0:SEQ - jb * P], PR[r, 13, jb * P:(jb + 1) * P], PR[r, 12, jb * P:SEQ],
                       start=True, stop=True).then_inc(sc_full, 1)

                ret_scores(0)
                for j in range(16):
                    h, jb = j // 4, j % 4
                    if j < 15:
                        ret_scores(j + 1)
                    pe.wait_ge(st_ready, std.up())
                    mm(M[64 * (h % 2):64 * (h % 2) + 64, 2 + h // 2, jb * P:SEQ], VR[:, jb, 64 * h:64 * h + 64],
                       AT[:, j % 2, 0:SEQ - jb * P], start=jb == 0, stop=jb == 3).then_inc(st_used, 1)
                for m in range(2):
                    pe.wait_ge(o_sb, osb.up())
                    mm(M[:, m, :], blk, PR[:, 12 + m, :], start=True, stop=True).then_inc(mean_full, 1)
                for m in range(2):
                    pe.wait_ge(osq_ready, osq.up())
                    mm(M[:, m, :], blk, sq[:, m, 0:SEQ], start=True, stop=True).then_inc(ovar_full, 1)
                pe.wait_ge(rg_ready, rg.up(2))
                for m in range(2):
                    pe.wait_ge(pooled, pol.up())
                    settle(pe)
                    for g in range(2):
                        r = slice(64 * g, 64 * g + 64)
                        ins = mm(M[r, m, :], par[r, C_PW + 64 * m:C_PW + 64 * m + 64], WS[r, m, 0, :], start=True, stop=True)
                    ins.then_inc(pool_full, 1)
                pe.wait_ge(ml_ready, mlr.up(4))

                def scores(u):
                    b, h, i = u % 2, u // 4, u % 4
                    pe.wait_ge(exp_ready, exf.up())
                    for m in range(2):
                        r = slice(64 * m, 64 * m + 64)
                        ins = mm(acc[b][:, m, 0:(i + 1) * P], PR[r, h, i * P:(i + 1) * P], PR[r, 4 + h, 0:(i + 1) * P],
                                 start=True, stop=True)
                    ins.then_inc(sc_full, 1)

                def transposes(u):
                    pe.wait_ge(a_ready, ar.up())
                    pe.wait_ge(at_ready, atf.up())
                    for k in range(u % 4 + 1):
                        ins = nc.tensor.transpose(M[:, u % 2, k * P:(k + 1) * P], PB[:, u % 2, 0, k * P:(k + 1) * P], ident)
                    ins.then_inc(at_full, 1)

                def values(u):
                    h, i = u // 4, u % 4
                    pe.wait_ge(at_ready, atd.up())
                    if i == 0:
                        pe.wait_ge(o_evac, oef.up())
                    for k in range(i + 1):
                        ins = mm(M[:, 2 + h % 2, i * P:(i + 1) * P], VT[:, k, h * P:(h + 1) * P],
                                 AT[:, u % 2, k * P:(k + 1) * P], start=k == 0, stop=k == i)
                    ins.then_inc(av_done, 1)

                scores(0)
                for u in range(16):
                    if u < 15:
                        scores(u + 1)
                    transposes(u)
                    if u:
                        values(u - 1)
                values(15)
                for h in range(4):
                    pe.wait_ge(osq_ready, osq.up())
                    mm(M[:, h % 2, :], ones128, sq[:, h % 2, 0:SEQ], start=True, stop=True).then_inc(ovar_full, 1)
                pe.wait_ge(rg_ready, rg.up(4))
                pe.wait_ge(ml_ready, mlr.up(4))
                pe.wait_ge(exp_ready, exf.now() + 2)
                exd.up(16)

            def up_pairs(T):
                first_pair(T)
                with loop(pe, FT - 1, [(hi, 2), (lo, 2), (ev, 2)]):
                    for _ in range(2):
                        project(T)
                pe.wait_ge(ff_ready, ffr.up(FT))

            def layer1():
                pe.wait_ge(param_in, prm.up(32))
                first_pair(SEQ)
                with loop(pe, IN1 // 2 - 1, [(hi, 2), (lo, 2), (ev, 2)]):
                    for _ in range(2):
                        project(SEQ)
                pe.wait_ge(param_in, prm.up(16))
                mixer1()
                with loop(pe, OUT1 // 2, [(hi, 2), (lo, 2), (ev, 2)]):
                    for _ in range(2):
                        project(SEQ)
                stats(SEQ)
                up_pairs(SEQ)
                down(SEQ)
                stats(SEQ)

            def ffn2():
                up_pairs(TALL)
                down(TALL)

            def col(c0):
                return (0, c0) if c0 < 272 else (1, c0 - 272)

            def gated():
                all_evacuated()
                settle(pe)
                for t, (c0, n) in enumerate(TILES2):
                    mm(z_bank(t, n), LR[0:64, c0:c0 + n], par[0:64, G_W2:G_W2 + 512], start=True, stop=True).then_inc(z_full, 1)
                for t, (c0, n) in enumerate(TILES2):
                    pe.wait_ge(tr_done, trd.up())
                    for h in range(4):
                        ins = nc.tensor.transpose(M[0:n, 2 + t % 2, h * P:(h + 1) * P], PR2[:, 4 + h, c0:c0 + n], ident)
                    ins.then_inc(tr_full, 1)
                lgr.up(5)
                pe.wait_ge(lg_ready, lgr.now() + 2)
                pe.wait_ge(tr_done, trd.now() + 2)
                for dm in range(4):
                    d, mt = dm // 2, dm % 2
                    cm = K2_CB if d else K2_CF
                    if dm:
                        pe.wait_ge(e_used, eu.up())
                    for t, (c0, n) in enumerate(TILES2):
                        b, c = col(c0)
                        ins = mm(M[:, 2 * (dm % 2) + b, c:c + n], LG[0:n, t, d * 256 + mt * P:d * 256 + (mt + 1) * P],
                                 con[0:n, cm:cm + n], start=True, stop=True)
                    ins.then_inc(cum_full, 1)
                eu.up()
                pe.wait_ge(e_used, eu.now() + 1)
                for t, (c0, n) in enumerate(TILES2):
                    pe.wait_ge(tr_done, trd.up())
                    for dm in range(4):
                        ins = nc.tensor.transpose(M[0:n, t % 2, dm * P:(dm + 1) * P], KI[:, dm, c0:c0 + n], ident)
                    ins.then_inc(tr_full, 1)
                pe.wait_ge(tr_done, trd.now() + 2)
                chunks = [(0, META)] + [(META + 64 * i, 64) for i in range(8)]
                for mt in range(2):
                    for d in range(2):
                        dm = 2 * d + mt
                        settle(pe)
                        place = [(s + d, s, (s + d + 1) % 2 if s + d else 0) for s in range(8)]
                        for c, s, half in sorted(place, key=lambda a: a[2]):
                            t, n = (c + 1) // 2, chunks[c][1]
                            r = slice(64 * half, 64 * half + n)
                            if half and c == 2:
                                pe.wait_ge(pe_step, pes.up())
                                settle(pe)
                            for h in range(2):
                                ins = mm(M[64 * h:64 * h + 64, 2 * d + s // 4, (s % 4) * P:(s % 4 + 1) * P],
                                         LG[r, t, dm * P + 64 * h:dm * P + 64 * h + 64],
                                         VA[r, t, (2 * mt + h) * P:(2 * mt + h + 1) * P], start=True, stop=True)
                            if c == 7:
                                ins.then_inc(pe_step, 1)
                        ins.then_inc(kv_full, 1)
                    pe.wait_ge(state_ready, stt.up(2))
                    pe.wait_ge(go_evac, gev.up(2))

                    def att(t):
                        c0, n = TILES2[t]
                        pe.wait_ge(att_ready, atnf.up())
                        settle(pe)
                        for d in range(2):
                            for h in range(2):
                                r = slice(64 * h, 64 * h + 64)
                                ins = mm(M[0:n, 2 * (t % 2) + h, d * P:d * P + n], KI[r, 2 * d + mt, c0:c0 + n], QD[r, 2 * d + mt, c0:c0 + n],
                                         start=True, stop=True)
                        ins.then_inc(att_full, 1)

                    att(0)
                    for t, (c0, n) in enumerate(TILES2):
                        if t < 4:
                            att(t + 1)
                        pe.wait_ge(att_ready, atnd.up())
                        b, c = col(c0)
                        for d in range(2):
                            for h in range(2):
                                g = (2 * h + d) * P
                                ins = mm(acc[h][:, b, c:c + n], VA[0:n, t, (2 * mt + h) * P:(2 * mt + h + 1) * P],
                                         ATG[0:n, t % 2, g:g + n], start=d == 0 and t in (0, 3), stop=False,
                                         skip_group_check=True)
                        ins.then_inc(att_used, 1)
                    for d in range(2):
                        for s in range(8):
                            c0, n = chunks[s + 1 - d]
                            b, c = col(c0)
                            for h in range(2):
                                r = slice(64 * h, 64 * h + 64)
                                ins = mm(acc[h][:, b, c:c + n], SS[r, d, s * P:(s + 1) * P], QD[r, 2 * d + mt, c0:c0 + n],
                                         start=False, stop=d == 1 and s == 7, skip_group_check=True)
                    ins.then_inc(go_full, 1)
                for h in range(4):
                    pe.wait_ge(osq_ready, osq.up())
                    rows(M[:, 2 * (h % 2):2 * (h % 2) + 2, :], ones128, sq[:, h % 2, :]).then_inc(ovar_full, 1)

            def attention2():
                for j in range(5):
                    pe.wait_ge(osq_ready, osq.up())
                    rows(M[:, 2 * (j % 2):2 * (j % 2) + 2, :], blk, sq[:, j % 2, :]).then_inc(ovar_full, 1)
                pe.wait_ge(rg_ready, rg.up(9))
                pe.wait_ge(qn_ready, qn.up(5))
                for j in range(4):
                    pe.wait_ge(roped, rop.up())
                    rows(M[:, 2 * (j % 2):2 * (j % 2) + 2, :], con[:, K2_PQ:K2_PQ + P], PR2[:, 12 + j, :]).then_inc(rot_full, 1)
                for kv in range(2):
                    rop.up()
                    pe.wait_ge(roped, rop.now() + 1)
                    rows(M[:, 0:2, :], con[:, K2_E0 + kv * P:K2_E0 + (kv + 1) * P], PR2[:, 16, :])
                    rows(M[:, 2:4, :], con[:, K2_S0 + kv * P:K2_S0 + (kv + 1) * P], PR2[:, 16, :]).then_inc(rot_full, 1)
                pe.wait_ge(roped, rop.now() + 2)
                pe.wait_ge(tr_done, trd.up())
                for t, (c0, n) in enumerate(TILES2):
                    dst = M[0:n, 0, (t - 1) * P:t * P] if t else M[0:n, 1, 0:P]
                    ins = nc.tensor.transpose(dst, PR2[:, 17, c0:c0 + n], ident)
                ins.then_inc(tr_full, 1)
                pe.wait_ge(tr_done, trd.now() + 2)

                def scores(u):
                    b, i, h = u % 2, u // 8, u % 8
                    pe.wait_ge(exp_ready, exf.up())
                    r = slice(64 * (h % 2), 64 * (h % 2) + 64)
                    for a in range(2):
                        ins = mm(acc[b][0:QB, a, 0:HALF], PR2[r, 12 + h // 2, QB * i:QB * i + QB],
                                 K2[r, h // 4, HALF * a:HALF * a + HALF], start=True, stop=True)
                    ins.then_inc(sc_full, 1)

                def transposes(u):
                    pe.wait_ge(exp_ready, exd.up())
                    pe.wait_ge(at_ready, atf.up())
                    for t, (c0, n) in enumerate(TILES2):
                        ins = nc.tensor.transpose(M[0:n, u % 2, t * QB:(t + 1) * QB], PB2[0:QB, u % 2, c0:c0 + n],
                                                  con[0:QB, K_ID:K_ID + QB])
                    ins.then_inc(at_full, 1)

                def values(u):
                    i, h = u // 8, u % 8
                    pe.wait_ge(at_ready, atd.up())
                    if h == 0 and i >= 2:
                        pe.wait_ge(ml_ready, mlr.up())
                    for t, (c0, n) in enumerate(TILES2):
                        ins = mm(M[0:QB, 2 + i % 2, 64 * h:64 * h + 64], PT2[0:n, u % 2, t, :],
                                 VB[0:n, t, 64 * (h // 4):64 * (h // 4) + 64], start=t == 0, stop=t == 4)
                    ins.then_inc(av_done, 1)

                def out_transposes(i):
                    pe.wait_ge(ob_ready, obr.up())
                    for m in range(4):
                        ins = nc.tensor.transpose(M[:, 2 + i % 2, m * QB:(m + 1) * QB], OB[0:QB, i % 2, m * P:(m + 1) * P],
                                                  con[0:QB, K_ID:K_ID + QB])
                    ins.then_inc(ot_full, 1)

                pe.wait_ge(ml_ready, mlr.up(4))
                scores(0)
                for u in range(8 * NQB):
                    if u < 8 * NQB - 1:
                        scores(u + 1)
                    transposes(u)
                    if u:
                        values(u - 1)
                    if u > 8 and u % 8 == 3:
                        out_transposes(u // 8 - 1)
                values(8 * NQB - 1)
                out_transposes(NQB - 1)
                pe.wait_ge(ml_ready, mlr.up(2))
                pe.wait_ge(exp_ready, exf.now() + 2)

            def layer2():
                pe.wait_ge(param_in, prm.up(32))
                ffn2()
                first_pair(TALL)
                with loop(pe, 8, [(hi, 2), (lo, 2), (ev, 2)]):
                    for _ in range(2):
                        project(TALL)
                project(TALL)
                s = next_slot()
                multiply([([(0, xh, xl, 0)], s, TALL)])
                pe.wait_ge(param_in, prm.up(16))
                gated()
                attention2()
                with loop(pe, 4, [(hi, 6), (lo, 6), (ev, 6)]):
                    for a in range(2):
                        project(TALL)
                        project(TALL)
                        s = next_slot()
                        multiply([([(k, mh, ml, k) for k in range(4)], s, TALL),
                                  ([(k, mh, ml, k) for k in range(4, 8)], M[:, 2:4, :], TALL)])
                pe.wait_ge(ff_ready, ffr.up(KT))
                with loop(pe, KT // 2, [(hi, 2), (lo, 2), (ev, 2)]):
                    for _ in range(2):
                        project(TALL, yh, yl)
                ffn2()

            pe.wait_ge(consts_in, 1)
            run_layers(pe, layer1, layer2, (hi, lo, ev, ssn, rr, xhr, xlr, ffr, mlr, trd, lin, lexp, rop, stf, std, osb,
                                            osq, rg, pol, exf, ar, atf, atd, oef, lgr, eu, kvn, stt, atnf, atnd, gev, cen,
                                            qn, exd, obr, prm, pes))
            stats(TALL)


def shape_constants():
    f = np.float32
    ident = np.eye(P, dtype=f)
    ones = np.full((P, P), 1.0 / D, f)
    ones128 = np.full((P, P), 1.0 / P, f)
    blk = np.kron(np.eye(2, dtype=f), np.full((64, 64), 1.0 / 64, f))

    def rotary(width, rot, pos_angles):
        half = rot // 2
        perm, cos, sin = np.zeros((P, P), f), np.ones((P, pos_angles.shape[0]), f), np.zeros((P, pos_angles.shape[0]), f)
        for m in range(P):
            r = m % width
            if r < rot:
                i = r % half
                perm[m + half if r < half else m - half, m] = 1
                cos[m] = np.cos(pos_angles[:, i])
                sin[m] = np.sin(pos_angles[:, i]) * (-1 if r < half else 1)
        return perm, cos, sin

    def angles(theta, rot, pos):
        inv = f(theta) ** (-np.arange(0, rot, 2, dtype=f) / f(rot))
        return (pos.astype(f)[:, None] * inv[None, :]).astype(f)

    pos = np.arange(SEQ)
    pda, cda, sda = rotary(64, 16, angles(500000.0, 16, pos))
    prt, crt, srt = rotary(32, 32, angles(10000.0, 32, pos))
    caus = np.where(np.arange(P)[None, :] <= np.arange(P)[:, None], 0.0, -1e30).astype(f)
    w = np.array([2, 4, 8, 16])[(np.arange(2)[None, :] * 2 + np.arange(P)[:, None] // 64)]
    rec = (1.0 / np.minimum(np.arange(16)[None, None, :] + 1, w[:, :, None])).astype(f).reshape(P, 32)
    c1 = np.zeros((P, NC1), f)
    for at, a in ((K_ID, ident), (K_ONES, ones), (K_ONE128, ones128), (K_BLK, blk), (K_PDA, pda), (K_PR, prt),
                  (K_CAUS, caus), (K_CAUS + P, caus), (K_REC, rec), (K_REC + 32, (1.0 / w).astype(f))):
        c1[:, at:at + a.shape[1]] = a
    gamma = 1.0 - 2.0 ** (-5.0 - np.arange(4))
    diff = np.arange(SEQ)[None, :] - np.arange(P)[:, None]
    decay = np.stack([np.where(diff >= 0, np.exp(np.maximum(diff, 0) * np.log(g)), 0.0) * 32 ** -0.5 for g in gamma], 1)
    t1 = np.concatenate([cda, sda, crt, srt, decay.reshape(P, 4 * SEQ).astype(f)], 1)

    row, colp = np.repeat(np.arange(SEQ // 64), 64), np.tile(np.arange(64), SEQ // 64)
    a_row, a_col = angles(10000.0, 32, row), angles(10000.0, 32, colp)
    pq, cq, sq_ = np.zeros((P, P), f), np.ones((P, TALL), f), np.zeros((P, TALL), f)
    for m in range(P):
        i, first = m % 16, m % 32 < 16
        pq[m + 16 if first else m - 16, m] = 1
        ang = (a_row, a_col)[m % 64 // 32][:, i]
        cq[m, META:] = np.cos(ang)
        sq_[m, META:] = np.sin(ang) * (-1 if first else 1)
    both = [np.tile(ident[:, 64 * kv:64 * kv + 64], (1, 2)) for kv in range(2)]
    swapped = [np.tile(pq[:, 64 * kv:64 * kv + 64], (1, 2)) for kv in range(2)]
    s, t = np.arange(P)[:, None], np.arange(P)[None, :]
    fwd = ((s // 64 == t // 64) & (s <= t)).astype(f)
    bwd = ((s // 64 == t // 64) & (s >= t)).astype(f)
    c2 = np.zeros((P, NC2), f)
    for at, a in ((K_ID, ident), (K_ONES, ones), (K_ONE128, ones128), (K_BLK, blk), (K2_PQ, pq), (K2_E0, both[0]),
                  (K2_E1, both[1]), (K2_S0, swapped[0]), (K2_S1, swapped[1]), (K2_CF, fwd / 16), (K2_CB, bwd / 16)):
        c2[:, at:at + P] = a
    t2 = np.concatenate([cq, sq_, fwd, bwd, fwd, bwd], 1)
    c1p = np.zeros((P, NC2), f)
    c1p[:, :NC1] = c1
    return c1p, c2, t1.astype(f), t2.astype(f)


def lay_out(a):
    strips = np.zeros((STRIPS, P, KT, P), np.float32)
    n = 0

    def put(w, c, rows=None, at=0, width=P, cols=None):
        w = w[rows] if rows is not None else w
        k = w.shape[0] // P
        c0 = P * c if cols is None else cols
        strips[n, :, at:at + k, 0:width] = w[:, c0:c0 + width].reshape(k, P, width).transpose(1, 0, 2)

    def down(w):
        nonlocal n
        for c in range(KT):
            for j in range(3):
                put(w, c, slice(P * KT * j, min(FF, P * KT * (j + 1))))
                n += 1

    for l in range(LAYERS):
        for c in range(IN1):
            put(a["w_in"][l], c)
            n += 1
        for c in range(OUT1):
            put(a["w_out"][l], c)
            n += 1
        for c in range(FT):
            for half in range(2):
                put(a["w_up"][l], c + half * FT)
                n += 1
        down(a["w_down"][l])
    for l in range(LAYERS):
        def ffn(i):
            nonlocal n
            for c in range(FT):
                for w in ("ffn_w_gate_2", "ffn_w_up_2"):
                    put(a[w][l, i], c)
                    n += 1
            down(a["ffn_w_down_2"][l, i])

        ffn(0)
        w = a["w_in_2"][l]
        for c in range(12):
            put(w, c)
            n += 1
        put(w, 0, width=32, cols=12 * P)
        n += 1
        for c in range(6):
            put(w, 0, cols=12 * P + 32 + P * c)
            n += 1
        n += 1
        for c in range(KT):
            put(w, 0, cols=2336 + P * c)
            n += 1
            put(w, 0, cols=2336 + D + P * c)
            n += 1
            put(a["w_pa_2"][l], c)
            put(a["w_pb_2"][l], c, at=4)
            n += 1
        for c in range(KT):
            put(a["w_out_2"][l], c)
            n += 1
        ffn(1)
    assert n == STRIPS, (n, STRIPS)
    tiles = lambda v: v.reshape(v.shape[0], -1, P).transpose(0, 2, 1)
    p1, p2 = np.zeros((LAYERS, P, NP1), np.float32), np.zeros((LAYERS, P, NP2), np.float32)
    for at, name in ((C_PRE, "norm_mix_pre"), (C_POST, "norm_mix_post"), (C_SUB, "diff_subln"), (C_RETG, "ret_norm"),
                     (C_PSC, "pool_scale"), (C_MPRE, "norm_mlp_pre"), (C_MPOST, "norm_mlp_post"), (C_CB, "conv_b")):
        v = tiles(a[name])
        p1[:, :, at:at + v.shape[2]] = v
    for j in range(3):
        p1[:, :, C_CW + j * 2 * FT:C_CW + (j + 1) * 2 * FT] = tiles(a["conv_w"][:, j])
    for j, name in enumerate(("lambda_q1", "lambda_k1", "lambda_q2", "lambda_k2")):
        p1[:, 0:64, C_LAM + j] = a[name]
    for l in range(LAYERS):
        li = 0.8 - 0.6 * math.exp(-0.3 * l)
        p1[l, :, C_LINIT], p1[l, :, C_LINIT + 1] = li, 1.0 - li
    p1[:, :, C_PW:] = a["pool_w"].reshape(LAYERS, 2, P, 64).transpose(0, 2, 1, 3).reshape(LAYERS, P, P)
    p2[:, :, G_N:G_N + 24] = tiles(a["norm_gains_2"].reshape(LAYERS, 3 * D))
    p2[:, :, G_GN:G_GN + 4] = tiles(a["gla_gn_2"])
    for h in range(2):
        p2[:, 64 * h:64 * h + 64, G_QN] = a["q_norm_2"]
        p2[:, 64 * h:64 * h + 64, G_KN] = a["k_norm_2"]
    p2[:, :, G_BM:G_BM + 16] = tiles(a["b_merge_2"].reshape(LAYERS, 2 * D))
    for d in range(2):
        p2[:, 16 * d:16 * d + 16, G_W2 + 256 * d:G_W2 + 256 * (d + 1)] = a["gla_w2_2"][:, d]
        p2[:, 32, G_W2 + 256 * d:G_W2 + 256 * (d + 1)] = a["gla_b2_2"][:, d]
    x = np.ascontiguousarray(a["x"][0].T.reshape(KT, P, SEQ).transpose(1, 0, 2))
    meta = np.ascontiguousarray(a["meta_tokens_2"].T.reshape(KT, P, META).transpose(1, 0, 2))
    fnorm = np.ascontiguousarray(a["final_norm_2"].reshape(KT, P).T)
    return strips.reshape(STRIPS, P, SW), p1, p2, x, meta, fnorm


def kernel(**inputs):
    import concourse.bacc as _bacc
    from concourse.bass_utils import run_bass_kernel_spmd as _run

    a = {k: np.asarray(v) for k, v in inputs.items()}
    strips, p1, p2, x, meta, fnorm = lay_out(a)
    c1, c2, t1, t2 = shape_constants()
    nc = _bacc.Bacc("TRN2", target_bir_lowering=False, num_devices=1)
    arrays = {"weights": strips, "params1": p1, "params2": p2, "consts1": c1, "consts2": c2, "tables1": t1,
              "tables2": t2, "x_in": x, "meta_in": meta, "fnorm": fnorm}
    args = {k: nc.dram_tensor(k, v.shape, F32, kind="ExternalInput").ap() for k, v in arrays.items()}
    out = nc.dram_tensor("out", (P, KT, SEQ), F32, kind="ExternalOutput").ap()
    build(nc, out=out, **args)
    r = _run(nc, [arrays], core_ids=[0])
    y = r.results[0]["out"]
    return np.ascontiguousarray(np.asarray(y).transpose(1, 0, 2).reshape(D, SEQ).T)[None]
```
